# Optimizing a Trainium2 kernel written in Bass

```python
import math
import jax, jax.numpy as jnp
from jax import lax
import numpy as np

D_MODEL = 1024
BATCH = 1
SEQ = 512
DEPTH = 1

GRID_W = 64
CTX_LEN = 256
EPS = 1e-6

D_MIX = D_MODEL
D_GROUP = D_MIX // 4
CONV_A = 31
CHUNK_B = 128
HEADS_B = 4
HEAD_DIM_C = 64
HEADS_C = D_GROUP // HEAD_DIM_C
GROUPS_C = 2
STATE_C = 128
CONV_C = 5
CHUNK_C = 128
HEAD_DIM_D = 64
HEADS_D = D_GROUP // HEAD_DIM_D
LORA_W = 64
LORA_A = 64
LORA_G = 128
GN_EPS_D = 64e-5
N_KEYS = 128
N_EXPERTS = N_KEYS * N_KEYS
PEER_HEADS = 8
PEER_DK = 256
PEER_TOPK = 16
PEER_BLOCK = 128

C_XBC = D_GROUP + 2 * GROUPS_C * STATE_C
A_COLS = 2 * D_GROUP
B_COLS = 2 * D_GROUP
C_COLS = D_GROUP + C_XBC + 2 * HEADS_C
D_COLS = 3 * D_GROUP + 2 * LORA_W + 2 * LORA_A + LORA_G
OFF_B = A_COLS
OFF_C = OFF_B + B_COLS
OFF_D = OFF_C + C_COLS
IN_COLS = OFF_D + D_COLS

kernel_name = "hybrid_headgroup_diffusion_block"

def rmsnorm(x, g):
    xf = x.astype(jnp.float32)
    y = xf * lax.rsqrt(jnp.mean(xf * xf, -1, keepdims=True) + EPS)
    return (y * g).astype(x.dtype)

def layernorm(x, g, b, eps=1e-5):
    xf = x.astype(jnp.float32)
    mu = jnp.mean(xf, -1, keepdims=True)
    var = jnp.mean(jnp.square(xf - mu), -1, keepdims=True)
    return ((xf - mu) * lax.rsqrt(var + eps) * g + b).astype(x.dtype)

def modulate(h, shift, scale):
    return h * (1 + scale) + shift

def depthwise_conv(x, w, b):
    k = w.shape[0]
    y = lax.conv_general_dilated(x, w[:, None, :].astype(x.dtype), window_strides=(1,),
                                 padding=[((k - 1) // 2, (k - 1) // 2)],
                                 dimension_numbers=('NWC', 'WIO', 'NWC'),
                                 feature_group_count=x.shape[-1])
    return y + b.astype(x.dtype)

def sincos_2d(t_len):
    rows = t_len // GRID_W
    row = jnp.repeat(jnp.arange(rows), GRID_W).astype(jnp.float32)
    col = jnp.tile(jnp.arange(GRID_W), rows).astype(jnp.float32)
    q = D_MODEL // 4
    freq = 10000.0 ** (-jnp.arange(q, dtype=jnp.float32) / q)
    ar = row[:, None] * freq
    ac = col[:, None] * freq
    return jnp.concatenate([jnp.sin(ar), jnp.cos(ar), jnp.sin(ac), jnp.cos(ac)], -1)

def mixer_conformer(p, conv_w, conv_b, ln_g, ln_b):
    hg = p[..., :D_GROUP] * jax.nn.sigmoid(p[..., D_GROUP:])
    hg = depthwise_conv(hg, conv_w, conv_b)
    return jax.nn.silu(layernorm(hg, ln_g, ln_b))

def mixer_chunk_mlp(p, ln_g, ln_b, w_s, b_s):
    bsz, t_len, _ = p.shape
    u, v = p[..., :D_GROUP], p[..., D_GROUP:]
    v = layernorm(v, ln_g, ln_b)
    v = v.reshape(bsz, t_len // CHUNK_B, CHUNK_B, HEADS_B, D_GROUP // HEADS_B)
    mixed = jnp.einsum('hij,bcjhd->bcihd', w_s, v) + b_s.T[None, None, :, :, None]
    return u * mixed.reshape(bsz, t_len, D_GROUP)

def segsum_exp(a):
    l = a.shape[-1]
    xe = jnp.broadcast_to(a[..., :, None], a.shape + (l,))
    strict = jnp.tril(jnp.ones((l, l), bool), -1)
    ss = jnp.cumsum(jnp.where(strict, xe, 0.0), axis=-2)
    return jnp.where(jnp.tril(jnp.ones((l, l), bool)), jnp.exp(ss), 0.0)

def ssd_scan(xdt, da, bm, cm, init, emit):
    b, t_len, h, pd = xdt.shape
    nc = t_len // CHUNK_C
    xc = xdt.reshape(b, nc, CHUNK_C, h, pd)
    bc = bm.reshape(b, nc, CHUNK_C, h, -1)
    cc = cm.reshape(b, nc, CHUNK_C, h, -1)
    ac = da.reshape(b, nc, CHUNK_C, h).transpose(0, 3, 1, 2).astype(jnp.float32)
    a_cs = jnp.cumsum(ac, -1)
    decay_states = jnp.exp(a_cs[..., -1:] - a_cs)
    states = jnp.einsum('bclhn,bhcl,bclhp->bchpn', bc, decay_states, xc)
    states = jnp.concatenate([init[:, None].astype(states.dtype), states], 1)
    decay_chunk = segsum_exp(jnp.pad(a_cs[..., -1], ((0, 0), (0, 0), (1, 0))))
    new_states = jnp.einsum('bhzc,bchpn->bzhpn', decay_chunk, states)
    final = new_states[:, -1]
    if not emit:
        return None, final
    lmat = segsum_exp(ac)
    y_diag = jnp.einsum('bclhn,bcshn,bhcls,bcshp->bclhp', cc, bc, lmat, xc)
    y_off = jnp.einsum('bclhn,bchpn,bhcl->bclhp', cc, new_states[:, :-1], jnp.exp(a_cs))
    return (y_diag + y_off).reshape(b, t_len, h, pd), final

def mamba_prepare(p, conv_w, conv_b):
    b, t_len, _ = p.shape
    z = p[..., :D_GROUP]
    xbc = jax.nn.silu(depthwise_conv(p[..., D_GROUP:D_GROUP + C_XBC], conv_w, conv_b))
    dt_raw = p[..., D_GROUP + C_XBC:].reshape(b, t_len, 2, HEADS_C)
    xs = xbc[..., :D_GROUP].reshape(b, t_len, HEADS_C, HEAD_DIM_C)
    gs = GROUPS_C * STATE_C
    bm = xbc[..., D_GROUP:D_GROUP + gs].reshape(b, t_len, GROUPS_C, STATE_C)
    cm = xbc[..., D_GROUP + gs:].reshape(b, t_len, GROUPS_C, STATE_C)
    rep = HEADS_C // GROUPS_C
    return z, xs, jnp.repeat(bm, rep, 2), jnp.repeat(cm, rep, 2), dt_raw

def mamba_output(prep, y, d_skip, norm_g):
    z, xs, _, _, _ = prep
    b, t_len = xs.shape[:2]
    y = (y + d_skip[:, None] * xs).reshape(b, t_len, D_GROUP)
    return rmsnorm(y * jax.nn.silu(z), norm_g)

def mixer_mamba(pl, pc, conv_w, conv_b, dt_bias, a_log, d_skip, norm_g, emit_ctx):
    lat = mamba_prepare(pl, conv_w, conv_b)
    cx = mamba_prepare(pc, conv_w, conv_b)
    init = jnp.zeros((pl.shape[0], HEADS_C, HEAD_DIM_C, STATE_C), jnp.float32)
    yl, yc = [], []
    for d in range(2):
        flip = (lambda t: jnp.flip(t, 1)) if d == 1 else (lambda t: t)
        a_d = -jnp.exp(a_log[d])

        def ssd_args(prep):
            _, xs, bm, cm, dt_raw = prep
            dt = jax.nn.softplus(dt_raw[:, :, d].astype(jnp.float32) + dt_bias[d])
            return flip(xs * dt[..., None]), flip(dt * a_d), flip(bm), flip(cm)

        y_c, s_ctx = ssd_scan(*ssd_args(cx), init, emit_ctx)
        y_l, _ = ssd_scan(*ssd_args(lat), s_ctx, True)
        yl.append(flip(y_l))
        if emit_ctx:
            yc.append(flip(y_c))
    out_l = mamba_output(lat, yl[0] + yl[1], d_skip, norm_g)
    out_c = mamba_output(cx, yc[0] + yc[1], d_skip, norm_g) if emit_ctx else None
    return out_l, out_c

def shift_lerp(p, mu_prev, mu_next):
    prev = jnp.pad(p, ((0, 0), (1, 0), (0, 0)))[:, :-1]
    nxt = jnp.pad(p, ((0, 0), (0, 1), (0, 0)))[:, 1:]
    return p + mu_prev * (prev - p) + mu_next * (nxt - p)

def rwkv_prepare(p, mu_prev, mu_next, w0, w2, a0, a2, k_k, k_a):
    p = shift_lerp(p, mu_prev, mu_next)
    b, t_len, _ = p.shape
    heads = lambda t: t.reshape(t.shape[:-1] + (HEADS_D, HEAD_DIM_D))
    r = p[..., :D_GROUP]
    k = p[..., D_GROUP:2 * D_GROUP]
    v = p[..., 2 * D_GROUP:3 * D_GROUP]
    o = 3 * D_GROUP
    wd = p[..., o:o + 2 * LORA_W].reshape(b, t_len, 2, LORA_W)
    o += 2 * LORA_W
    ad = p[..., o:o + 2 * LORA_A].reshape(b, t_len, 2, LORA_A)
    o += 2 * LORA_A
    gd = p[..., o:]
    w = w0 + jnp.einsum('btdr,drc->btdc', jnp.tanh(wd), w2)
    decay = jnp.exp(-jnp.exp(-jax.nn.softplus(-w.astype(jnp.float32)) - 0.5))
    a = jax.nn.sigmoid(a0 + jnp.einsum('btdr,drc->btdc', ad, a2))
    kk = heads(k * k_k).astype(jnp.float32)
    kk = kk * lax.rsqrt(jnp.sum(kk * kk, -1, keepdims=True) + 1e-12)
    kd = k[:, :, None] * (1 + (a - 1) * k_a)
    return heads(r), heads(v), heads(decay), heads(a), kk, heads(kd), gd

def rwkv_scan(prep, d, init, reverse, emit):
    r, v, decay, a, kk, kd, _ = prep
    xs = (decay[:, :, d], kk, kk * a[:, :, d], kd[:, :, d], v) + ((r,) if emit else ())
    xs = tuple(jnp.moveaxis(t, 1, 0) for t in xs)

    def step(s, inp):
        w_t, kk_t, kka_t, k_t, v_t = inp[:5]
        s = (s * w_t[:, :, None, :]
             - jnp.einsum('bhvk,bhk->bhv', s, kk_t)[..., None] * kka_t[:, :, None, :]
             + v_t[..., None] * k_t[:, :, None, :])
        y = jnp.einsum('bhvk,bhk->bhv', s, inp[5]) if emit else None
        return s, y

    s, ys = lax.scan(step, init, xs, reverse=reverse)
    return s, (jnp.moveaxis(ys, 0, 1) if emit else None)

def rwkv_output(prep, y, g2, r_k, gn_g, gn_b):
    r, v, _, _, _, kd, gd = prep
    b, t_len = r.shape[:2]
    mu = jnp.mean(y, -1, keepdims=True)
    var = jnp.mean(jnp.square(y - mu), -1, keepdims=True)
    yn = ((y - mu) * lax.rsqrt(var + GN_EPS_D)).reshape(b, t_len, D_GROUP) * gn_g + gn_b
    bonus = jnp.sum(r[:, :, None] * kd * r_k, axis=(2, 4))[..., None] * v
    g = jax.nn.sigmoid(gd) @ g2
    return (yn + bonus.reshape(b, t_len, D_GROUP)) * g

def mixer_rwkv(pl, pc, mu_prev, mu_next, w0, w2, a0, a2, g2, k_k, k_a, r_k, gn_g, gn_b, emit_ctx):
    lat = rwkv_prepare(pl, mu_prev, mu_next, w0, w2, a0, a2, k_k, k_a)
    cx = rwkv_prepare(pc, mu_prev, mu_next, w0, w2, a0, a2, k_k, k_a)
    init = jnp.zeros((pl.shape[0], HEADS_D, HEAD_DIM_D, HEAD_DIM_D), jnp.float32)
    yl, yc = [], []
    for d in range(2):
        s_ctx, y_c = rwkv_scan(cx, d, init, d == 1, emit_ctx)
        _, y_l = rwkv_scan(lat, d, s_ctx, d == 1, True)
        yl.append(y_l)
        if emit_ctx:
            yc.append(y_c)
    out_l = rwkv_output(lat, yl[0] + yl[1], g2, r_k, gn_g, gn_b)
    out_c = rwkv_output(cx, yc[0] + yc[1], g2, r_k, gn_g, gn_b) if emit_ctx else None
    return out_l, out_c

def peer_ffn(f, wq, k1, k2, u_tab, v_tab):
    b, t_len, _ = f.shape
    blocks = f.reshape(-1, PEER_BLOCK, D_MODEL)
    nc = PEER_TOPK * PEER_TOPK

    def block(fb):
        q = (fb @ wq).reshape(PEER_BLOCK, PEER_HEADS, 2, PEER_DK // 2)
        s1 = jnp.einsum('thd,kd->thk', q[:, :, 0], k1).astype(jnp.float32)
        s2 = jnp.einsum('thd,kd->thk', q[:, :, 1], k2).astype(jnp.float32)
        v1, i1 = lax.top_k(s1, PEER_TOPK)
        v2, i2 = lax.top_k(s2, PEER_TOPK)
        cand = (v1[..., :, None] + v2[..., None, :]).reshape(PEER_BLOCK, PEER_HEADS, nc)
        cand_idx = (i1[..., :, None] * N_KEYS + i2[..., None, :]).reshape(PEER_BLOCK, PEER_HEADS, nc)
        top, pos = lax.top_k(cand, PEER_TOPK)
        idx = jnp.take_along_axis(cand_idx, pos, axis=-1)
        gate = jax.nn.softmax(top, axis=-1)
        act = jax.nn.gelu(jnp.einsum('thkd,td->thk', u_tab[idx], fb)) * gate
        return jnp.einsum('thk,thkd->td', act, v_tab[idx])

    return lax.map(block, blocks).reshape(b, t_len, D_MODEL)

def setup_inputs(seed: int = 0) -> dict:
    key = jax.random.key(seed)
    ks = iter(jax.random.split(key, 64))
    f32 = jnp.float32
    L = DEPTH

    def nrm(shape, scale=1.0):
        return jax.random.normal(next(ks), shape, f32) * scale

    def gain(shape):
        return 1.0 + nrm(shape, 0.05)

    def unif(shape, lo, hi):
        return jax.random.uniform(next(ks), shape, f32, lo, hi)

    dt = jnp.exp(unif((L, 2, HEADS_C), math.log(1e-3), math.log(1e-1)))
    return {
        'x': nrm((BATCH, SEQ, D_MODEL)),
        'c': nrm((BATCH, D_MODEL)),
        'ctx': nrm((BATCH, CTX_LEN, D_MODEL)),
        'c_ctx': nrm((D_MODEL,)),
        'ada_w': nrm((L, D_MODEL, 6 * D_MODEL), 0.5 * D_MODEL ** -0.5),
        'ada_b': nrm((L, 6 * D_MODEL), 0.02),
        'norm_mix_g': gain((L, D_MODEL)),
        'norm_ffn_g': gain((L, D_MODEL)),
        'w_in': nrm((L, D_MODEL, IN_COLS), D_MODEL ** -0.5),
        'w_out': nrm((L, D_MIX, D_MODEL), D_MIX ** -0.5),
        'a_conv_w': nrm((L, CONV_A, D_GROUP), CONV_A ** -0.5),
        'a_conv_b': nrm((L, D_GROUP), 0.02),
        'a_ln_g': gain((L, D_GROUP)),
        'a_ln_b': nrm((L, D_GROUP), 0.02),
        'b_ln_g': gain((L, D_GROUP)),
        'b_ln_b': nrm((L, D_GROUP), 0.02),
        'b_ws': nrm((L, HEADS_B, CHUNK_B, CHUNK_B), CHUNK_B ** -0.5),
        'b_bs': gain((L, HEADS_B, CHUNK_B)),
        'c_conv_w': nrm((L, CONV_C, C_XBC), CONV_C ** -0.5),
        'c_conv_b': nrm((L, C_XBC), 0.02),
        'c_dt_bias': dt + jnp.log(-jnp.expm1(-dt)),
        'c_a_log': jnp.log(unif((L, 2, HEADS_C), 1.0, 16.0)),
        'c_d': 1.0 + nrm((L, HEADS_C), 0.1),
        'c_norm_g': gain((L, D_GROUP)),
        'd_mu_prev': unif((L, D_COLS), 0.0, 0.5),
        'd_mu_next': unif((L, D_COLS), 0.0, 0.5),
        'd_w0': nrm((L, 2, D_GROUP), 0.5),
        'd_w2': nrm((L, 2, LORA_W, D_GROUP), 0.1),
        'd_a0': nrm((L, 2, D_GROUP), 0.5),
        'd_a2': nrm((L, 2, LORA_A, D_GROUP), 0.1),
        'd_g2': nrm((L, LORA_G, D_GROUP), LORA_G ** -0.5),
        'd_k_k': 0.85 + nrm((L, D_GROUP), 0.05),
        'd_k_a': gain((L, D_GROUP)),
        'd_r_k': nrm((L, HEADS_D, HEAD_DIM_D), 0.1),
        'd_gn_g': gain((L, D_GROUP)),
        'd_gn_b': nrm((L, D_GROUP), 0.02),
        'peer_wq': nrm((L, D_MODEL, PEER_HEADS * PEER_DK), D_MODEL ** -0.5),
        'peer_k1': nrm((L, N_KEYS, PEER_DK // 2), (PEER_DK // 2) ** -0.5),
        'peer_k2': nrm((L, N_KEYS, PEER_DK // 2), (PEER_DK // 2) ** -0.5),
        'peer_u': nrm((L, N_EXPERTS, D_MODEL), D_MODEL ** -0.5),
        'peer_v': nrm((L, N_EXPERTS, D_MODEL), 0.5),
        'final_g': gain((D_MODEL,)),
    }

def reference(x, c, ctx, c_ctx, ada_w, ada_b, norm_mix_g, norm_ffn_g, w_in, w_out,
              a_conv_w, a_conv_b, a_ln_g, a_ln_b, b_ln_g, b_ln_b, b_ws, b_bs,
              c_conv_w, c_conv_b, c_dt_bias, c_a_log, c_d, c_norm_g,
              d_mu_prev, d_mu_next, d_w0, d_w2, d_a0, d_a2, d_g2, d_k_k, d_k_a, d_r_k,
              d_gn_g, d_gn_b, peer_wq, peer_k1, peer_k2, peer_u, peer_v, final_g):
    h = x + sincos_2d(x.shape[1]).astype(x.dtype)
    hc = ctx
    for i in range(DEPTH):
        emit = i < DEPTH - 1
        m = (jax.nn.silu(c) @ ada_w[i] + ada_b[i]).reshape(c.shape[0], 6, 1, D_MODEL)
        mc = (jax.nn.silu(c_ctx) @ ada_w[i] + ada_b[i]).reshape(6, 1, D_MODEL)
        col0 = 0 if emit else OFF_C
        pl = modulate(rmsnorm(h, norm_mix_g[i]), m[:, 0], m[:, 1]) @ w_in[i]
        pc = modulate(rmsnorm(hc, norm_mix_g[i]), mc[0], mc[1]) @ w_in[i][:, col0:]
        y_a = mixer_conformer(pl[..., :OFF_B], a_conv_w[i], a_conv_b[i], a_ln_g[i], a_ln_b[i])
        y_b = mixer_chunk_mlp(pl[..., OFF_B:OFF_C], b_ln_g[i], b_ln_b[i], b_ws[i], b_bs[i])
        y_c, yc_c = mixer_mamba(pl[..., OFF_C:OFF_D], pc[..., OFF_C - col0:OFF_D - col0],
                                c_conv_w[i], c_conv_b[i], c_dt_bias[i], c_a_log[i], c_d[i],
                                c_norm_g[i], emit)
        y_d, yc_d = mixer_rwkv(pl[..., OFF_D:], pc[..., OFF_D - col0:], d_mu_prev[i], d_mu_next[i],
                               d_w0[i], d_w2[i], d_a0[i], d_a2[i], d_g2[i], d_k_k[i], d_k_a[i],
                               d_r_k[i], d_gn_g[i], d_gn_b[i], emit)
        h = h + m[:, 2] * (jnp.concatenate([y_a, y_b, y_c, y_d], -1) @ w_out[i])
        f = modulate(rmsnorm(h, norm_ffn_g[i]), m[:, 3], m[:, 4])
        h = h + m[:, 5] * peer_ffn(f, peer_wq[i], peer_k1[i], peer_k2[i], peer_u[i], peer_v[i])
        if emit:
            yc_a = mixer_conformer(pc[..., :OFF_B], a_conv_w[i], a_conv_b[i], a_ln_g[i], a_ln_b[i])
            yc_b = mixer_chunk_mlp(pc[..., OFF_B:OFF_C], b_ln_g[i], b_ln_b[i], b_ws[i], b_bs[i])
            hc = hc + mc[2] * (jnp.concatenate([yc_a, yc_b, yc_c, yc_d], -1) @ w_out[i])
            fc = modulate(rmsnorm(hc, norm_ffn_g[i]), mc[3], mc[4])
            hc = hc + mc[5] * peer_ffn(fc, peer_wq[i], peer_k1[i], peer_k2[i], peer_u[i], peer_v[i])
    return rmsnorm(h, final_g)


_drawn_inputs = setup_inputs


def setup_inputs(seed=0):
    import zlib

    import numpy as np

    out = dict(_drawn_inputs(seed))
    spreads = {}
    factors = {'ctx': 8.0,
     'c_ctx': 8.0,
     'norm_mix_g': 2.847,
     'norm_ffn_g': 15.641,
     'a_conv_b': 35.64,
     'a_ln_g': 56.547,
     'a_ln_b': 64.0,
     'b_ln_g': 6.672,
     'b_ln_b': 34.602,
     'b_bs': 6.538,
     'c_conv_b': 43.526,
     'c_a_log': 3.969,
     'c_d': 58.792,
     'c_norm_g': 40.387,
     'd_w2': 3.694,
     'd_a0': 3.209,
     'd_k_k': 60.848,
     'd_k_a': 5.018,
     'd_gn_g': 64.0,
     'd_gn_b': 200.0}
    for name, (base, spread) in spreads.items():
        noise = np.random.default_rng([zlib.crc32(name.encode()), seed]).standard_normal(out[name].shape)
        drawn = base * np.exp(spread * noise) if base else spread * noise
        out[name] = __import__('jax').numpy.asarray(drawn.astype(out[name].dtype))
    for name, factor in factors.items():
        out[name] = (out[name] * factor).astype(out[name].dtype)
    return out
```

```python
from contextlib import ExitStack

import numpy as np
import concourse.bass as bass
from concourse import mybir

F32 = mybir.dt.float32
U32 = mybir.dt.uint32
U8 = mybir.dt.uint8
ALU = mybir.AluOpType
ACT = mybir.ActivationFunctionType
AX = mybir.AxisListType

P = 128
D = 1024
KT = D // P
SEQ, CTX = 512, 256
NLAT, NCTX = SEQ // P, CTX // P
NTILE = NLAT + NCTX
TOK = SEQ + CTX
EPS = 1e-6
OFF_B, OFF_C, OFF_D = 512, 1024, 2056
TAPS_A, TAPS_C = 31, 5
HEADS = 4
LOGW = float(np.exp(-0.5))
PH, TOPK, NKEY, NEXP = 8, 16, 128, 16384
LEVELS = 7

COL_TILES = ([(128 * j, "a") for j in range(4)] + [(OFF_B + 128 * j, "u") for j in range(2)]
             + [(OFF_B + 256 + 128 * j, "v") for j in range(2)]
             + [(OFF_C + 256 + 128 * j, "c") for j in range(6)]
             + [(OFF_C + 128 * j, "z") for j in range(2)]
             + [(OFF_D + 128 * j, "d") for j in range(9)])
DT_AFTER = 13

BETWEEN = {(14, 0): ["a_tok"], (15, 0): ["dt_exp"], (16, 1): ["c_silu"], (17, 0): ["c_tok", "a_std"],
           (18, 0): ["a_back", "b_std"], (18, 1): ["c_decay"], (19, 0): ["b_mix"], (19, 1): ["G0", "state0"],
           (20, 0): ["state1"], (20, 1): ["Y0", "G1"], (21, 0): ["state2"], (21, 1): ["Y1", "G2"],
           (22, 0): ["state3"], (22, 1): ["Y2", "G3"], (23, 0): ["state4"], (23, 1): ["Y3"], (24, 0): ["state5"]}

COLS = {}
_n = 0
for _name, _c in (("mixg", 8), ("acw", 62), ("acb", 2), ("alg", 2), ("alb", 2), ("ccw", 30), ("ccb", 6),
                  ("mup", 9), ("mun", 9), ("w0", 4), ("a0", 4), ("kk", 2), ("ka", 2), ("rk", 2),
                  ("gng", 2), ("gnb", 2), ("cng", 2)):
    COLS[_name] = (_n, _c)
    _n += _c
NCOL = _n
ROWS = {"blg": (0, 256), "blb": (256, 256), "dtb": (512, 8), "alog": (520, 8), "cd": (528, 4)}
NROW = 532

IDENT, LT, LE, GT, GE, NLT, NLE, NGT, NGE, ONES, BLK, KEY1, KEY2 = range(13)
NMAT = 11


def build_program(nc, A, out):
    ctx = ExitStack()
    with ctx:
        sem_cache = {}

        def sem(name):
            if name not in sem_cache:
                sem_cache[name] = ctx.enter_context(nc.semaphore(name))
            return sem_cache[name]

        arena = ctx.enter_context(nc.sbuf_tensor("arena", [P, 200 * 256], F32))
        levels = ctx.enter_context(nc.sbuf_tensor("levels", [P, 2 * LEVELS, P], U8))
        psum = ctx.enter_context(nc.psum_tensor("psum", [P, 8 * 512], F32))
        h_dram = nc.dram_tensor("h_scratch", (SEQ, D), F32, kind="Internal").ap()
        h2_dram = nc.dram_tensor("h2_scratch", (SEQ, D), F32, kind="Internal").ap()

        def at(kb, *shape):
            n = int(np.prod(shape))
            v = arena[:, int(kb * 256):int(kb * 256) + n]
            names = "abcd"[:len(shape)]
            if len(shape) == 1:
                return v
            return v.rearrange(f"p ({' '.join(names)}) -> p {' '.join(names)}",
                               **{k: s for k, s in zip(names, shape)})

        def bank(b, *shape):
            n = int(np.prod(shape)) if shape else 512
            v = psum[:, b * 512:b * 512 + n]
            if len(shape) < 2:
                return v
            names = "abcd"[:len(shape)]
            return v.rearrange(f"p ({' '.join(names)}) -> p {' '.join(names)}",
                               **{k: s for k, s in zip(names, shape)})

        mats = at(0, 14, P)
        mat = lambda i: mats[:, i, :]
        scanm = at(9, TOK)
        cols = at(12, NCOL)
        col = lambda name, j=0: cols[:, COLS[name][0] + j:COLS[name][0] + j + 1]
        colr = lambda name: cols[:, COLS[name][0]:COLS[name][0] + COLS[name][1]]
        yT = at(13, 8, SEQ)
        small = at(29, 768)
        csil = small[:, 0:16].rearrange("p (k s) -> p k s", s=2)
        modcol = small[:, 16:48].rearrange("p (k s) -> p k s", s=2)
        gcol = small[:, 48:64].rearrange("p (k s) -> p k s", s=2)
        stat = small[:, 64:80]
        eps_c = small[:, 80:84]
        kam1 = small[:, 84:86]
        cmid = small[:, 720:732].rearrange("p (c g) -> p c g", c=2)
        mumid = small[:, 86:95]
        dts = small[:, 96:144]
        das = small[:, 144:192]
        tmp48 = small[:, 192:240]
        decs = small[:, 240:480].rearrange("p (m n) -> p m n", m=5)
        cst = small[:, 480:528]
        aneg = small[:, 528:536]
        qa = small[:, 536:560].rearrange("p (d c g) -> p d c g", d=2, c=2)
        qb = small[:, 560:584].rearrange("p (d c g) -> p d c g", d=2, c=2)
        qs = small[:, 584:608].rearrange("p (d c g) -> p d c g", d=2, c=2)
        lnst = small[:, 608:672].rearrange("p (a b) -> p a b", a=4)
        tmp48b = small[:, 672:720]

        Dp = at(32, 9, 772)
        Dsh = at(60, 9, TOK)
        Xst = [at(k, D) for k in (48, 52, 56, 60, 64, 68)]
        Pst = [at(k, D) for k in (72, 76, 80, 154)]
        XN = [at(179 + 4 * i, D) for i in range(2)]
        sqs = at(158, D)
        levels_f = at(163, 2 * LEVELS, P)
        adaA = [at(32, KT, 512), at(127, KT, 512)]
        silA = at(146, KT, P)
        modA = at(171, 4, 512)
        XT = at(87, KT, TOK)
        wring = [at(111 + 4 * i, KT, P) for i in range(4)]
        Cp = at(127, 6, 776)
        Araw = at(146, 4, SEQ)
        zt = at(154, NLAT, 256)
        vt = at(158, NLAT, 256)
        ut = at(162, 2, SEQ)
        Apad = at(166, 2, 542)
        Cx = at(171, 6, TOK)
        rows = at(189, NROW)
        bsb = at(191.5, 2, P)
        wsT = at(192.5, HEADS, P)
        wdt = at(194.5, KT, 8)
        w2s = at(195, 256)
        a2s = at(196, 256)
        g2s = at(197, 256)
        Ah = at(146, 2, SEQ)
        At = at(150, NLAT, 256)
        Asq = at(166, NLAT, 256)
        Bsq = at(166, NLAT, 256)
        Bmix = at(139, 2, NLAT, P)
        xs_t = at(60, NTILE, 256)
        B_t = at(66, NTILE, 256)
        xdt = [at(72 + 4 * d, NLAT, 256) for d in range(2)]
        Lm = [at(80 + 2 * i, HEADS, P) for i in range(2)]
        Sc = [at(84 + d, 256) for d in range(2)]
        Ctmp = at(86, 256)
        xst = [at(127 + 6 * d, NTILE, 256) for d in range(2)]
        seg = [at(139 + 2 * i, HEADS, P) for i in range(2)]
        Gm = [at(146 + 4 * d, NLAT, 2, P) for d in range(2)]
        Csq = at(158, NLAT, 256)
        yC = at(166, NLAT, 256)
        sw = at(32, 2, TOK)
        cen = at(38, 2, TOK)
        Wx = at(44, 2, TOK)
        Ex = at(50, 2, TOK)
        kds = at(56, 2, SEQ)
        aA = at(87, 2, TOK)
        kdA = at(99, 2, TOK)
        kkA = at(105, 2, TOK)
        AR = [at(111 + 12 * d, 2, NTILE, 2, P) for d in range(2)]
        Bt = [at(135 + 6 * d, 2, TOK) for d in range(2)]
        Kt = [at(147 + 6 * d, 2, TOK) for d in range(2)]
        base = (159, 87)
        KAR = [at(base[d], 2, 2, 256) for d in range(2)]
        BAR = [at(base[d] + 4, 2, 2, 256) for d in range(2)]
        NA = [at(base[d] + 8, 2, 2, P) for d in range(2)]
        Xi = [at(base[d] + 10, 2, 2, P) for d in range(2)]
        Yi = [at(base[d] + 12, 2, 2, P) for d in range(2)]
        Ri = [at(base[d] + 14, 2, 2, P) for d in range(2)]
        Vt = at(175, NTILE, 256)
        KB = [at(181 + 2 * d, 2, 256) for d in range(2)]
        Zs = [at(103 + d, 256) for d in range(2)]
        SAs = [at(105 + d, 256) for d in range(2)]
        Zst = [at(107 + d, 2, P) for d in range(2)]
        T1 = [at(109 + d, 2, P) for d in range(2)]
        yD = at(32, NLAT, 256)
        gD = at(36, 2, SEQ)
        bon = at(40, 2, SEQ)
        Dsq = at(44, NLAT, 256)
        rkA = at(48, 2, SEQ)
        w_o = at(32, KT, D)
        hL = at(64, NLAT, D)
        zrhs = at(0, 512)
        modBn = at(80, 8, 512)
        modB = at(80, 4, D)
        rowG = at(96, D)
        f_tok = at(104, NLAT, D)
        fT = at(120, KT, P)
        silB = at(120, KT, P)
        wqr = [at(104 + 4 * i, D) for i in range(3)]
        adaB = [at(124, KT, 512), at(140, KT, 512)]
        Wp = at(124, KT, 2048)
        ytmp = at(188, 512)
        osq = at(190, D)
        s_all = at(64, NLAT, PH, 2, P)
        Ur = [at(32 + 4 * i, D) for i in range(8)]
        Vr = [at(k, D) for k in (13, 17, 21, 25, 188, 192, 196, 100)]
        gate2 = at(96, D)
        accS = at(124, NLAT, D)
        hfin = at(140, NLAT, D)
        rowF = at(156, D)
        fsq = at(160, D)

        def own(name, shape, dt=F32):
            return ctx.enter_context(nc.sbuf_tensor(name, shape, dt))

        NH = NLAT * PH
        iota16 = own("iota16", [P, 16])
        dots = own("dots", [P, 16])
        gel = own("gel", [P, 16])
        egate = own("egate", [P, 16])
        esum = own("esum", [P, 2])
        act_cur = own("act_cur", [P, 16])
        zmat_t = own("zmat", [P, P])
        zmat = zmat_t[:, :]
        diag = at(7, 2, P)
        idx_all = own("idx_all", [P, NH * 16], U32)
        act_all = at(9, NH * 16)
        top_all = at(11, NH * 16)
        idxU = own("idxU", [P, 2, 16], U32)
        idxV = own("idxV", [P, 2, 16], U32)
        sc = at(8, 2, P)
        sc2 = at(31, 2, P)
        v16 = own("v16", [P, 2, 16])
        i16 = own("i16", [P, 2, 16], U32)
        i16f = own("i16f", [P, 2, 16])
        cand = at(5, 256)
        cand2 = at(6, 256)
        oh = at(3, 2, 256)
        top16 = own("top16", [P, 16])
        pos = own("pos", [P, 16], U32)
        posab = own("posab", [P, 2, 16], U32)
        posf = own("posf", [P, 2, 16])
        sel = own("sel", [P, 2, 16])

        class Engine:

            def __init__(self, eng, name):
                self.e, self.n, self.done = eng, 0, sem(f"{name}_done")

            def do(self, ins):
                self.n += 1
                ins.then_inc(self.done, 1)

            def sync(self):
                self.e.wait_ge(self.done, self.n)

            def step(self, ins):
                self.do(ins)
                self.sync()

        bank_full = [sem(f"bank_full{b}") for b in range(8)]
        bank_free = [sem(f"bank_free{b}") for b in range(8)]
        uses, owed, use_of = [0] * 8, [0] * 8, {}
        freed = [0] * 8

        def take(pe, name, b, readers=1):
            if owed[b]:
                pe.wait_ge(bank_free[b], owed[b])
            uses[b] += 1
            owed[b] += readers
            use_of[name] = (b, uses[b])
            return b

        def full(e, name):
            b, k = use_of[name]
            e.wait_ge(bank_full[b], k)
            return b

        def give(ins, b):
            ins.then_inc(bank_full[b], 1)

        block = ctx.enter_context(nc.Block())
        ORDER = [[0, 1, 2, 3, 4, 5], [1, 0, 5, 4, 3, 2]]
        fL = float(P)

        @block.tensor
        def _(pe):
            def mm(o, l, r, start=True, stop=True, **k):
                return pe.matmul(o, l, r, start=start, stop=stop, **k)

            def tr(o, i):
                return pe.transpose(o, i, mat(IDENT))

            pe.wait_ge(sem("consts"), 16)
            pe.wait_ge(sem("iota"), 2)
            pe.wait_ge(sem("sil_a"), 1)
            for n in range(4):
                b = take(pe, f"adaA{n}", n % 2)
                pe.wait_ge(sem(f"ada_slot{n % 2}"), 16 * (n // 2 + 1))
                for k in range(KT):
                    last = mm(bank(b), silA[:, k, :], adaA[n % 2][:, k, :], k == 0, k == KT - 1)
                give(last, b)
            for n in range(4):
                b = take(pe, f"mc{n}", 2 + n)
                pe.wait_ge(sem("mod_a"), n + 1)
                for j in range(4):
                    last = tr(bank(b)[:, j * P:(j + 1) * P], modA[:, n, j * P:(j + 1) * P])
                give(last, b)
            for g in range(NTILE):
                pe.wait_ge(sem("xn"), g + 1)
                for q in range(2):
                    b = take(pe, f"xt{g}{q}", (2 * g + q) % 8)
                    for j in range(4):
                        k = 4 * q + j
                        last = tr(bank(b)[:, j * P:(j + 1) * P], XN[g % 2][:, k * P:(k + 1) * P])
                    give(last, b)

            def a_tok():
                pe.wait_ge(sem("a_conv"), 1)
                for t in range(2):
                    b = take(pe, f"at{t}", 5 + t)
                    for i in range(NLAT):
                        last = tr(bank(b)[:, i * P:(i + 1) * P], Ah[:, t, i * P:(i + 1) * P])
                    give(last, b)

            def a_back():
                pe.wait_ge(sem("a_norm"), 1)
                for t in range(2):
                    b = take(pe, f"ab{t}", 6 + t)
                    for i in range(NLAT):
                        last = tr(bank(b)[:, i * P:(i + 1) * P], At[:, i, t * P:(t + 1) * P])
                    give(last, b)

            def b_mix():
                pe.wait_ge(sem("b_norm"), 1)
                for t in range(2):
                    b = take(pe, f"bm{t}", 4 + t)
                    for i in range(NLAT):
                        for hp in range(2):
                            h = 2 * t + hp
                            last = mm(bank(b)[64 * hp:64 * hp + 64, i * P:(i + 1) * P],
                                      vt[:, i, h * 64:(h + 1) * 64], wsT[:, h, :])
                    give(last, b)

            def c_tok():
                pe.wait_ge(sem("c_conv"), 1)
                for t in range(4):
                    for q in range(2):
                        b = take(pe, f"ct{t}{q}", 4 + (2 * t + q) % 4)
                        for gg in range(3):
                            g = 3 * q + gg
                            last = tr(bank(b)[:, gg * P:(gg + 1) * P], Cx[:, t, g * P:(g + 1) * P])
                        give(last, b)

            def c_decay():
                pe.wait_ge(sem("c_da"), 1)
                b = take(pe, "dec", 6)
                for m, which in enumerate((LE, GT, GE, LT, ONES)):
                    last = mm(bank(b)[:, m * 48:(m + 1) * 48], mat(which), das)
                give(last, b)

            def chunk_scores(i):
                b = take(pe, f"G{i}", 4 + i % 2)
                sl = slice(CTX + i * P, CTX + (i + 1) * P)
                for gr in range(2):
                    last = mm(bank(b)[:, gr * P:(gr + 1) * P], Cx[:, 2 + gr, sl], Cx[:, 4 + gr, sl])
                give(last, b)
                for d in range(2):
                    n = 2 * i + d
                    pe.wait_ge(sem("c_segrhs"), n + 1)
                    b = take(pe, f"seg{n}", 6 + d)
                    give(mm(bank(b), mat((GT, LT)[d]), seg[d].rearrange("p a b -> p (a b)")), b)

            def chunk_outputs(i):
                b = take(pe, f"yc{i}", 4 + i % 2)
                pe.wait_ge(sem("c_M"), 2 * i + 2)
                for h in range(HEADS):
                    for d in range(2):
                        last = mm(bank(b)[:, h * 64:(h + 1) * 64], Lm[d][:, h, :],
                                  xdt[d][:, i, h * 64:(h + 1) * 64], d == 0, d == 1)
                give(last, b)

            def chunk_state(step):
                for d in range(2):
                    g = ORDER[d][step]
                    if g >= NCTX:
                        pe.wait_ge(sem(f"c_state{d}"), step)
                        b = take(pe, f"yo{d}{g}", 4 + d)
                        for gr in range(2):
                            last = mm(bank(b)[:, gr * P:(gr + 1) * P], Cx[:, 4 + gr, g * P:(g + 1) * P],
                                      Sc[d][:, gr * P:(gr + 1) * P])
                        give(last, b)
                    if step < NTILE - 1:
                        if step == 0:
                            pe.wait_ge(sem("c_xst"), 1)
                        b = take(pe, f"cu{d}{step}", 6 + d)
                        for gr in range(2):
                            last = mm(bank(b)[:, gr * P:(gr + 1) * P], B_t[:, g, gr * P:(gr + 1) * P],
                                      xst[d][:, g, gr * P:(gr + 1) * P])
                        give(last, b)

            def between(j, part):
                for name in BETWEEN.get((j, part), ()):
                    if name == "a_tok":
                        a_tok()
                    elif name == "a_back":
                        a_back()
                    elif name == "b_mix":
                        b_mix()
                    elif name == "c_tok":
                        c_tok()
                    elif name == "c_decay":
                        c_decay()
                    elif name[0] == "G":
                        chunk_scores(int(name[1]))
                    elif name[0] == "Y":
                        chunk_outputs(int(name[1]))
                    elif name[:5] == "state":
                        chunk_state(int(name[5]))

            pe.wait_ge(sem("xt_ready"), 2 * NTILE)
            pe.wait_ge(sem("params"), 16 * 7)
            for j, (_, part) in enumerate(COL_TILES):
                w = wring[j % 4]
                pe.wait_ge(sem(f"w_slot{j % 4}"), 16 * (j // 4 + 1))
                b = take(pe, f"p{j}", j % 2)
                if part in "zv":
                    for i in range(NLAT):
                        for k in range(KT):
                            last = mm(bank(b)[:, i * P:(i + 1) * P], XT[:, k, CTX + i * P:CTX + (i + 1) * P],
                                      w[:, k, :], k == 0, k == KT - 1)
                else:
                    for k in range(KT):
                        last = mm(bank(b), w[:, k, :], XT[:, k, CTX:], k == 0, k == KT - 1)
                give(last, b)
                between(j, 0)
                if part in "cd":
                    b = take(pe, f"pc{j}", 2 + j % 2)
                    for k in range(KT):
                        last = mm(bank(b)[:, 0:CTX], w[:, k, :], XT[:, k, 0:CTX], k == 0, k == KT - 1)
                    give(last, b)
                    between(j, 1)
                if j == DT_AFTER:
                    b = take(pe, "dt", 4)
                    for g in range(NTILE):
                        for k in range(KT):
                            last = mm(bank(b)[:, g * 8:g * 8 + 8], XT[:, k, g * P:(g + 1) * P], wdt[:, k, :],
                                      k == 0, k == KT - 1)
                    give(last, b)
            pe.wait_ge(sem("c_norm"), 1)
            for t in range(2):
                b = take(pe, f"cb{t}", 6 + t)
                for i in range(NLAT):
                    last = tr(bank(b)[:, i * P:(i + 1) * P], yC[:, i, t * P:(t + 1) * P])
                give(last, b)
            pe.wait_ge(sem("d_tanh"), 1)
            n = 0
            for d in range(2):
                for kind, wt, src in (("w", w2s, 6), ("a", a2s, 7)):
                    for t in range(2):
                        b0, b1 = 2 * (n % 4), 2 * (n % 4) + 1
                        take(pe, f"l{kind}{d}{t}", b0)
                        give(mm(bank(b0), wt[64 * d:64 * d + 64, t * P:(t + 1) * P],
                                Dsh[64 * d:64 * d + 64, src, CTX:]), b0)
                        take(pe, f"lc{kind}{d}{t}", b1)
                        give(mm(bank(b1)[:, 0:CTX], wt[64 * d:64 * d + 64, t * P:(t + 1) * P],
                                Dsh[64 * d:64 * d + 64, src, 0:CTX]), b1)
                        n += 1
                if d == 0:
                    pe.wait_ge(sem("d_kksq"), 1)
                    for t in range(2):
                        b0, b1 = 2 * (n % 4), 2 * (n % 4) + 1
                        take(pe, f"kn{t}", b0)
                        give(mm(bank(b0), mat(BLK), Ex[:, t, CTX:]), b0)
                        take(pe, f"knc{t}", b1)
                        give(mm(bank(b1)[:, 0:CTX], mat(BLK), Ex[:, t, 0:CTX]), b1)
                        n += 1
            for g in range(NTILE):
                if g % 2 == 0:
                    b = take(pe, f"vt{g // 2}", 2 * (g // 2))
                for t in range(2):
                    o = ((g % 2) * 2 + t) * P
                    last = tr(bank(b)[:, o:o + P], Dsh[:, 4 + t, g * P:(g + 1) * P])
                if g % 2:
                    give(last, b)
            pe.wait_ge(sem("d_prep"), 2)
            for r in range(NTILE):
                for d in range(2):
                    g = ORDER[d][r]
                    tk = slice(g * P, (g + 1) * P)
                    for hp in range(2):
                        hs = slice(64 * hp, 64 * hp + 64)
                        take(pe, f"kar{r}{d}{hp}", hp)
                        for t in range(2):
                            last = mm(bank(hp)[:, t * 256:(t + 1) * 256], Kt[d][hs, t, tk],
                                      AR[d][hs, t, g, :, :].rearrange("p a b -> p (a b)"))
                        give(last, hp)
                    for hp in range(2):
                        hs = slice(64 * hp, 64 * hp + 64)
                        take(pe, f"bar{r}{d}{hp}", 2 + hp)
                        for t in range(2):
                            last = mm(bank(2 + hp)[:, t * 256:(t + 1) * 256], Bt[d][hs, t, tk],
                                      AR[d][hs, t, g, :, :].rearrange("p a b -> p (a b)"))
                        give(last, 2 + hp)
                    for hp in range(2):
                        hs = slice(64 * hp, 64 * hp + 64)
                        take(pe, f"na{r}{d}{hp}", 4 + hp)
                        for t in range(2):
                            last = mm(bank(4 + hp)[:, t * P:(t + 1) * P], AR[d][hs, t, g, 0, :], Bt[d][hs, t, tk])
                        give(last, 4 + hp)
                    b = take(pe, f"kbt{r}{d}", 6 + d)
                    for t in range(2):
                        tr(bank(b)[:, t * P:(t + 1) * P], Kt[d][:, t, tk])
                    for t in range(2):
                        last = tr(bank(b)[:, (2 + t) * P:(3 + t) * P], Bt[d][:, t, tk])
                    give(last, b)
                for lv in range(1, LEVELS):
                    for d in range(2):
                        pe.wait_ge(sem(f"inv{d}"), LEVELS * r + lv)
                        b = take(pe, f"R{r}{d}{lv}", 3 * d)
                        for q in range(4):
                            last = mm(bank(b)[:, q * P:(q + 1) * P], NA[d][:, q // 2, q % 2, :],
                                      Yi[d][:, q // 2, q % 2, :])
                        give(last, b)
                    for d in range(2):
                        pe.wait_ge(sem(f"invR{d}"), (LEVELS - 1) * r + lv)
                        if lv < LEVELS - 1:
                            b = take(pe, f"PX{r}{d}{lv}", 3 * d + 1)
                            for q in range(4):
                                last = mm(bank(b)[:, q * P:(q + 1) * P], Ri[d][:, q // 2, q % 2, :],
                                          Xi[d][:, q // 2, q % 2, :])
                            give(last, b)
                        b = take(pe, f"PY{r}{d}{lv}", 3 * d + 2)
                        for q in range(4):
                            last = mm(bank(b)[:, q * P:(q + 1) * P], Xi[d][:, q // 2, q % 2, :],
                                      Ri[d][:, q // 2, q % 2, :])
                        give(last, b)
                for d in range(2):
                    g = ORDER[d][r]
                    tk = slice(g * P, (g + 1) * P)
                    b = take(pe, f"Z{r}{d}", 6 + d)
                    if r > 0:
                        pe.wait_ge(sem(f"d_state{d}"), r)
                    pe.wait_ge(sem("d_vt"), 3)
                    for t in range(2):
                        if r > 0:
                            mm(bank(b)[:, t * P:(t + 1) * P], AR[d][:, t, g, 0, :], Zst[d][:, t, :], True, False,
                               skip_group_check=True)
                        for hp in range(2):
                            h = 2 * t + hp
                            last = mm(bank(b)[:, h * 64:(h + 1) * 64], KAR[d][:, hp, t, 0:P],
                                      Vt[:, g, h * 64:(h + 1) * 64], r == 0, True, skip_group_check=r > 0)
                    give(last, b)
                for d in range(2):
                    pe.wait_ge(sem(f"d_Z{d}"), r + 1)
                    pe.wait_ge(sem(f"inv{d}"), LEVELS * (r + 1))
                    b = take(pe, f"SA{r}{d}", 6 + d)
                    for h in range(4):
                        last = mm(bank(b)[:, h * 64:(h + 1) * 64], Yi[d][:, h % 2, h // 2, :],
                                  Zs[d][:, h * 64:(h + 1) * 64])
                    give(last, b)
                for d in range(2):
                    g = ORDER[d][r]
                    pe.wait_ge(sem(f"d_SA{d}"), r + 1)
                    pe.wait_ge(sem(f"d_KB{d}"), r + 1)
                    b = take(pe, f"YU{r}{d}", 6 + d)
                    if g >= NCTX:
                        for t in range(2):
                            mm(bank(b)[:, t * P:(t + 1) * P], AR[d][:, t, g, 1, :], Zst[d][:, t, :], True, False,
                               skip_group_check=True)
                            for hp in range(2):
                                h = 2 * t + hp
                                mm(bank(b)[:, h * 64:(h + 1) * 64], KAR[d][:, hp, t, P:2 * P],
                                   Vt[:, g, h * 64:(h + 1) * 64], False, False, skip_group_check=True)
                                last = mm(bank(b)[:, h * 64:(h + 1) * 64], BAR[d][:, hp, t, P:2 * P],
                                          SAs[d][:, h * 64:(h + 1) * 64], False, True, skip_group_check=True)
                    if r < NTILE - 1:
                        for t in range(2):
                            mm(bank(b)[:, 256 + t * P:256 + (t + 1) * P], KB[d][:, 0, t * P:(t + 1) * P],
                               Vt[:, g, t * P:(t + 1) * P], True, False)
                            last = mm(bank(b)[:, 256 + t * P:256 + (t + 1) * P], KB[d][:, 1, t * P:(t + 1) * P],
                                      SAs[d][:, t * P:(t + 1) * P], False, True)
                    give(last, b)
            pe.wait_ge(sem("d_rk"), 1)
            for t in range(2):
                b = take(pe, f"bon{t}", t)
                give(mm(bank(b), mat(BLK), rkA[:, t, :]), b)
                b = take(pe, f"gate{t}", 2 + t)
                give(mm(bank(b), g2s[:, t * P:(t + 1) * P], Dsh[:, 8, CTX:]), b)
            pe.wait_ge(sem("d_gn"), 1)
            for t in range(2):
                b = take(pe, f"db{t}", 4 + t)
                for i in range(NLAT):
                    last = tr(bank(b)[:, i * P:(i + 1) * P], yD[:, i, t * P:(t + 1) * P])
                give(last, b)
            pe.wait_ge(sem("sil_b"), 1)
            for n in range(8):
                b = take(pe, f"adaB{n}", n % 2)
                pe.wait_ge(sem(f"adaB_slot{n % 2}"), 16 * (n // 2 + 1))
                for k in range(KT):
                    last = mm(bank(b), silB[:, k, :], adaB[n % 2][:, k, :], k == 0, k == KT - 1)
                give(last, b)
            pe.wait_ge(sem("keys"), 32)
            for hh in range(16):
                pe.wait_ge(sem(f"wq_slot{hh % 3}"), 16 * (hh // 3 + 1))
                for q in range(2):
                    b = take(pe, f"wp{hh}{q}", 2 + (2 * hh + q) % 4)
                    for j in range(4):
                        k = 4 * q + j
                        last = mm(bank(b)[:, j * P:(j + 1) * P], wqr[hh % 3][:, k * P:(k + 1) * P],
                                  mat(KEY1 + hh % 2))
                    give(last, b)
            pe.wait_ge(sem("w_out"), 16)
            pe.wait_ge(sem("y_done"), 4)
            for i in range(NLAT):
                for q in range(2):
                    b = take(pe, f"o{i}{q}", (2 * i + q) % 4)
                    for k in range(KT):
                        last = mm(bank(b), yT[:, k, i * P:(i + 1) * P], w_o[:, k, q * 512:(q + 1) * 512],
                                  k == 0, k == KT - 1)
                    give(last, b)
            for i in range(NLAT):
                pe.wait_ge(sem("f_ready"), i + 1)
                for q in range(2):
                    b = take(pe, f"ft{i}{q}", 4 + q)
                    for j in range(4):
                        k = 4 * q + j
                        last = tr(bank(b)[:, j * P:(j + 1) * P], f_tok[:, i, k * P:(k + 1) * P])
                    give(last, b)
                pe.wait_ge(sem("fT_ready"), 2 * (i + 1))
                for n in range(4):
                    b = take(pe, f"s{i}{n}", 6 + n % 2)
                    for k in range(KT):
                        last = mm(bank(b), fT[:, k, :], Wp[:, k, n * 512:(n + 1) * 512], k == 0, k == KT - 1)
                    give(last, b)
            for i in range(NLAT):
                b0 = 2 * (i % 2)
                for q in range(2):
                    take(pe, f"acc{i}{q}", b0 + q)
                    mm(bank(b0 + q), zmat, zrhs, True, False, skip_group_check=True)
                with pe.Fori(0, PH) as h:
                    for s in range(TOPK):
                        pe.wait_ge(sem("diag_ready"), h * TOPK + (i * PH * TOPK + s + 1))
                        pe.wait_ge(sem(f"v_slot{s % 8}"), h * 32 + (i * PH * 32 + 16 * (s // 8 + 1)))
                        mm(bank(b0), diag[:, s % 2, :], Vr[s % 8][:, 0:512], False, False, skip_group_check=True)
                        mm(bank(b0 + 1), diag[:, s % 2, :], Vr[s % 8][:, 512:], False, False,
                           skip_group_check=True).then_inc(sem("v_used"), 1)
                for q in range(2):
                    give(mm(bank(b0 + q), zmat, zrhs, False, True, skip_group_check=True), b0 + q)

        @block.sync
        def _(sp):
            def ld(dst, src, s):
                sp.dma_start(dst, src).then_inc(sem(s), 16)

            ld(mats[:, 0:NMAT, :], A["mats"], "consts")
            ld(csil, A["cc"], "cc")
            ld(cols, A["cols"], "cols")
            ld(Xst[0], A["ctx"][0:P, :], "x0")
            ld(adaA[0], A["ada_w"][0], "ada_slot0")
            ld(Xst[1], A["ctx"][P:2 * P, :], "x1")
            ld(adaA[1], A["ada_w"][1], "ada_slot1")
            ld(modA, A["adab_a"], "adab")
            for g in range(2, NTILE):
                ld(Xst[g], A["x"][(g - 2) * P:(g - 1) * P, :], f"x{g}")
                ld(Pst[g - 2], A["pos"][(g - 2) * P:(g - 1) * P, :], f"x{g}")
            for n in (2, 3):
                b, k = use_of[f"adaA{n - 2}"]
                sp.wait_ge(bank_full[b], k)
                ld(adaA[n % 2], A["ada_w"][n], f"ada_slot{n % 2}")
            ld(rows, A["rows"], "params")
            ld(bsb, A["bsb"], "params")
            ld(wsT, A["wsT"], "params")
            ld(wdt, A["wdt"], "params")
            ld(w2s, A["w2"], "params")
            ld(a2s, A["a2"], "params")
            ld(g2s, A["g2"], "params")
            ld(levels_f, A["levels"], "levels")
            ld(mats[:, KEY1, :], A["k1T"], "keys")
            ld(mats[:, KEY2, :], A["k2T"], "keys")
            for g in range(2, NTILE):
                sp.wait_ge(sem("h_sum"), g - 1)
                sp.dma_start(h_dram[(g - 2) * P:(g - 1) * P, :], Xst[g]).then_inc(sem("h_saved"), 16)
            for j in range(len(COL_TILES)):
                if j >= 4:
                    pr = COL_TILES[j - 4][1]
                    b, k = use_of[f"pc{j - 4}" if pr in "cd" else f"p{j - 4}"]
                    sp.wait_ge(bank_full[b], k)
                ld(wring[j % 4], A["w_in"][j], f"w_slot{j % 4}")
            sp.wait_ge(sem("d_rounds"), 1)
            ld(adaB[0], A["ada_w"][4], "adaB_slot0")
            ld(adaB[1], A["ada_w"][5], "adaB_slot1")
            sp.wait_ge(sem("y_done"), 4)
            ld(modBn, A["adab_b"], "adab_b")
            ld(rowG, A["ffn_g"], "ffn_g")
            ld(w_o, A["w_out"], "w_out")
            sp.wait_ge(sem("h_saved"), 16 * NLAT)
            ld(hL, h_dram.rearrange("(i p) d -> p i d", p=P), "h_load")
            for n in range(2, 8):
                b, k = use_of[f"adaB{n - 2}"]
                sp.wait_ge(bank_full[b], k)
                ld(adaB[n % 2], A["ada_w"][4 + n], f"adaB_slot{n % 2}")
            for hh in range(16):
                if hh >= 3:
                    b, k = use_of[f"wp{hh - 3}1"]
                    sp.wait_ge(bank_full[b], k)
                ld(wqr[hh % 3], A["wqT"][hh], f"wq_slot{hh % 3}")
            for i in range(NLAT):
                sp.wait_ge(sem("h2_ready"), i + 1)
                sp.dma_start(h2_dram[i * P:(i + 1) * P, :], hL[:, i, :]).then_inc(sem("h2_saved"), 16)
            sp.wait_ge(sem("h2_saved"), 16 * NLAT)
            sp.wait_ge(sem("s_ready"), 4 * NLAT)
            ld(hfin, h2_dram.rearrange("(i p) d -> p i d", p=P), "hfin")
            ld(rowF, A["fin_g"], "hfin")
            for i in range(NLAT):
                sp.wait_ge(sem("out_tile"), i + 1)
                sp.dma_start(out[i * P:(i + 1) * P, :], hfin[:, i, :]).then_inc(sem("out_saved"), 16)
            sp.wait_ge(sem("out_saved"), 16 * NLAT)

        @block.scalar
        def _(e):
            a = Engine(e, "act")
            act = e.activation

            def free(b):
                e.sem_inc(bank_free[b], 1)

            def signal(name):
                e.sem_inc(sem(name), 1)

            nstd = [0]

            def std(o, i, scale, eps):
                nstd[0] += 1
                e.wait_ge(sem("var_ready"), nstd[0])
                a.step(act(o, i, ACT.Sqrt, scale=scale, bias=eps))
                signal("std_ready")

            e.wait_ge(sem("cc"), 16)
            a.step(act(csil, csil, ACT.Silu))
            signal("csil")
            e.wait_ge(sem("eps"), 4)
            e.wait_ge(sem("cols"), 16)
            for g in range(NTILE):
                if g < NCTX:
                    e.wait_ge(sem(f"x{g}"), 16)
                else:
                    e.wait_ge(sem("h_sum"), g - 1)
                a.step(act(sqs, Xst[g], ACT.Square, accum_out=stat[:, g:g + 1]))
            a.step(act(stat[:, 8:8 + NTILE], stat[:, 0:NTILE], ACT.Sqrt, scale=1.0 / D, bias=eps_c[:, 0:1]))
            signal("x_std")
            e.wait_ge(sem("gcol"), 1)
            for g in range(NTILE):
                c = 1 if g < NCTX else 0
                for q in range(2):
                    b = full(e, f"xt{g}{q}")
                    for j in range(4):
                        k = 4 * q + j
                        a.do(act(XT[:, k, g * P:(g + 1) * P], bank(b)[:, j * P:(j + 1) * P], ACT.Identity,
                                 scale=gcol[:, k, c:c + 1], bias=modcol[:, k, c:c + 1]))
                    a.sync()
                    free(b)
                    signal("xt_ready")

            def between(j, part):
                for name in BETWEEN.get((j, part), ()):
                    if name == "a_tok":
                        for t in range(2):
                            b = full(e, f"at{t}")
                            a.step(act(At[:, :, t * P:(t + 1) * P], bank(b, NLAT, P), ACT.Copy))
                            free(b)
                        signal("a_tok")
                    elif name == "dt_exp":
                        e.wait_ge(sem("dt_abs"), 1)
                        a.step(act(tmp48b, tmp48b, ACT.Exp, scale=-1.0))
                        a.step(act(aneg, rows[:, 520:528], ACT.Exp))
                        signal("dt_exp")
                    elif name == "c_silu":
                        e.wait_ge(sem("c_taps"), 1)
                        for t in range(6):
                            a.do(act(Cx[:, t, :], Cx[:, t, :], ACT.Silu, bias=col("ccb", t)))
                        a.sync()
                        signal("c_conv")
                    elif name == "c_tok":
                        for t in range(4):
                            dst = (xs_t if t < 2 else B_t)
                            for q in range(2):
                                b = full(e, f"ct{t}{q}")
                                a.step(act(dst[:, 3 * q:3 * q + 3, (t % 2) * P:(t % 2 + 1) * P], bank(b, 3, P),
                                           ACT.Copy))
                                free(b)
                        signal("c_tok")
                    elif name == "a_std":
                        std(lnst[:, 1, 0:4], lnst[:, 0, 0:4], 1.0 / 256, eps_c[:, 3:4])
                    elif name == "a_back":
                        for t in range(2):
                            b = full(e, f"ab{t}")
                            a.step(act(yT[:, t, :], bank(b), ACT.Silu, scale=col("alg", t), bias=col("alb", t)))
                            free(b)
                        signal("y_done")
                    elif name == "b_std":
                        std(lnst[:, 1, 0:4], lnst[:, 0, 0:4], 1.0 / 256, eps_c[:, 3:4])
                        e.wait_ge(sem("dt_1p"), 1)
                        a.step(act(tmp48b, tmp48b, ACT.Ln))
                        signal("dt_ln")
                    elif name == "c_decay":
                        b = full(e, "dec")
                        a.step(act(decs, bank(b)[:, 0:240].rearrange("p (m n) -> p m n", m=5), ACT.Exp))
                        free(b)
                        signal("c_dec")
                    elif name[0] == "G":
                        i = int(name[1])
                        for d in range(2):
                            b = full(e, f"seg{2 * i + d}")
                            if i >= 1:
                                full(e, f"yc{i - 1}")
                            a.step(act(Lm[d], bank(b, HEADS, P), ACT.Exp))
                            free(b)
                            signal("c_L")

            e.wait_ge(sem("pads"), 1)
            e.wait_ge(sem("params"), 16 * 7)
            for j, (_, part) in enumerate(COL_TILES):
                b = full(e, f"p{j}")
                if part == "a":
                    a.step(act(Araw[:, j, :], bank(b), ACT.Sigmoid if j >= 2 else ACT.Copy))
                elif part == "u":
                    a.step(act(ut[:, j - 4, :], bank(b), ACT.Copy))
                elif part in "zv":
                    t = (j - 6) if part == "v" else (j - 14)
                    dst = (vt if part == "v" else zt)[:, :, t * P:(t + 1) * P]
                    a.step(act(dst, bank(b, NLAT, P), ACT.Copy if part == "v" else ACT.Silu))
                elif part == "c":
                    a.step(act(Cp[:, j - 8, 262:774], bank(b), ACT.Copy))
                else:
                    a.step(act(Dp[:, j - 16, 259:771], bank(b), ACT.Copy))
                free(b)
                if part not in "cd":
                    signal("part_" + part)
                between(j, 0)
                if part in "cd":
                    b = full(e, f"pc{j}")
                    if part == "c":
                        a.step(act(Cp[:, j - 8, 2:258], bank(b)[:, 0:CTX], ACT.Copy))
                    else:
                        a.step(act(Dp[:, j - 16, 1:257], bank(b)[:, 0:CTX], ACT.Copy))
                    free(b)
                    signal("part_" + part)
                    between(j, 1)
            std(lnst[:, 1, 0:4], lnst[:, 0, 0:4], 1.0 / 256, eps_c[:, 0:1])
            for t in range(2):
                b = full(e, f"cb{t}")
                a.step(act(yT[:, 4 + t, :], bank(b), ACT.Copy, scale=col("cng", t)))
                free(b)
            signal("y_done")
            e.wait_ge(sem("d_shift"), 1)
            a.step(act(Dsh[:, 6, :], Dsh[:, 6, :], ACT.Tanh))
            a.step(act(Dsh[:, 8, :], Dsh[:, 8, :], ACT.Sigmoid))
            signal("d_tanh")
            for d in range(2):
                if d == 1:
                    e.wait_ge(sem("d_prep"), 1)
                for kind, dst, bias in (("w", sw, "w0"), ("a", aA, "a0")):
                    for t in range(2):
                        b = full(e, f"l{kind}{d}{t}")
                        a.step(act(dst[:, t, CTX:], bank(b), ACT.Sigmoid, bias=col(bias, 2 * d + t)))
                        free(b)
                        b = full(e, f"lc{kind}{d}{t}")
                        a.step(act(dst[:, t, 0:CTX], bank(b)[:, 0:CTX], ACT.Sigmoid, bias=col(bias, 2 * d + t)))
                        free(b)
                signal("d_sw")
                if d == 0:
                    e.wait_ge(sem("d_kksq"), 1)
                    for t in range(2):
                        b = full(e, f"kn{t}")
                        a.step(act(Wx[:, t, CTX:], bank(b), ACT.Sqrt, bias=eps_c[:, 1:2]))
                        free(b)
                        b = full(e, f"knc{t}")
                        a.step(act(Wx[:, t, 0:CTX], bank(b)[:, 0:CTX], ACT.Sqrt, bias=eps_c[:, 1:2]))
                        free(b)
                    signal("d_kkn")
                e.wait_ge(sem("d_cen"), d + 1)
                wv = Wx.rearrange("p c (g t) -> p c g t", g=NTILE)
                cv = cen.rearrange("p c (g t) -> p c g t", g=NTILE)
                a.step(act(qa[:, d], wv[:, :, :, 0], ACT.Exp, scale=LOGW))
                a.step(act(qb[:, d], cv[:, :, :, P - 1], ACT.Exp, scale=-LOGW))
                for n, (src, sg) in enumerate(((Wx, -LOGW), (cen, -LOGW), (cen, LOGW)) if d == 0 else
                                              ((cen, LOGW), (Wx, LOGW), (Wx, -LOGW))):
                    if 3 * d + n:
                        e.wait_ge(sem("d_exused"), 3 * d + n)
                    a.step(act(Ex, src, ACT.Exp, scale=sg))
                    signal("d_ex")
            for q in range(3):
                b = full(e, f"vt{q}")
                a.step(act(Vt[:, 2 * q:2 * q + 2, :], bank(b, 2, 256), ACT.Copy))
                free(b)
                signal("d_vt")
            for r in range(NTILE):
                for d in range(2):
                    b = full(e, f"kbt{r}{d}")
                    a.do(act(KB[d][:, 0, :], bank(b)[:, 0:256], ACT.Copy))
                    a.do(act(KB[d][:, 1, :], bank(b)[:, 256:512], ACT.Copy, scale=-1.0))
                    a.sync()
                    free(b)
                    signal(f"d_KB{d}")
                for lv in range(1, LEVELS):
                    for d in range(2):
                        b = full(e, f"R{r}{d}{lv}")
                        a.step(act(Ri[d].rearrange("p a b c -> p (a b c)"), bank(b), ACT.Copy))
                        free(b)
                        signal(f"invR{d}")
                for d in range(2):
                    b = full(e, f"Z{r}{d}")
                    a.step(act(Zs[d], bank(b)[:, 0:256], ACT.Copy))
                    free(b)
                    signal(f"d_Z{d}")
                for d in range(2):
                    b = full(e, f"SA{r}{d}")
                    a.step(act(SAs[d], bank(b)[:, 0:256], ACT.Copy))
                    free(b)
                    signal(f"d_SA{d}")
            for t in range(2):
                b = full(e, f"gate{t}")
                a.step(act(gD[:, t, :], bank(b), ACT.Copy))
                free(b)
            signal("d_gate")
            std(lnst[:, 1, :], lnst[:, 0, :], 1.0 / 64, eps_c[:, 2:3])
            for t in range(2):
                b = full(e, f"db{t}")
                a.step(act(yT[:, 6 + t, :], bank(b), ACT.Identity, scale=col("gng", t), bias=col("gnb", t)))
                free(b)
            signal("d_back")
            for n in range(8):
                full(e, f"adaB{n}")
            for hh in range(16):
                for q in range(2):
                    b = full(e, f"wp{hh}{q}")
                    a.step(act(Wp[:, 4 * q:4 * q + 4, hh * P:(hh + 1) * P], bank(b, 4, P), ACT.Copy))
                    free(b)
            signal("wp_ready")
            for i in range(NLAT):
                e.wait_ge(sem("h2_ready"), i + 1)
                a.step(act(osq, hL[:, i, :], ACT.Square, accum_out=stat[:, i:i + 1]))
                a.step(act(stat[:, 8 + i:9 + i], stat[:, i:i + 1], ACT.Sqrt, scale=1.0 / D, bias=eps_c[:, 0:1]))
                signal("f_std")
            for i in range(NLAT):
                for q in range(2):
                    b = full(e, f"ft{i}{q}")
                    a.step(act(fT[:, 4 * q:4 * q + 4, :], bank(b, 4, P), ACT.Copy))
                    free(b)
                    signal("fT_ready")
                if i == 0:
                    e.wait_ge(sem("h2_saved"), 16 * NLAT)
                    e.wait_ge(sem("f_ready"), NLAT)
                for n in range(4):
                    b = full(e, f"s{i}{n}")
                    a.step(act(s_all[:, i, 2 * n:2 * n + 2, :, :].rearrange("p a b c -> p (a b c)"), bank(b), ACT.Copy))
                    free(b)
                    signal("s_ready")

            def gates(n):
                e.wait_ge(sem("u_used"), n * TOPK + TOPK)
                act(gel[:, :], dots[:, :], ACT.Gelu_apprx_tanh).then_inc(sem("gates"), 1)
                act(egate[:, :], top_all[:, bass.ds(n * 16, 16)], ACT.Exp, accum_out=esum[:, 0:1])\
                    .then_inc(sem("gates"), 1)

            def diagonals(n):
                e.wait_ge(sem("act_ready"), n + 1)
                act(act_cur[:, :], act_all[:, bass.ds(n * 16, 16)], ACT.Copy).then_inc(sem("cur"), 1)
                e.wait_ge(sem("cur"), n + 1)
                for s in range(TOPK):
                    if s >= 2:
                        e.wait_ge(sem("v_used"), n * TOPK + (s - 1))
                    act(diag[:, s % 2, :], mat(IDENT), ACT.Copy, scale=act_cur[:, s:s + 1])\
                        .then_inc(sem("diag_ready"), 1)
                e.wait_ge(sem("v_used"), n * TOPK + TOPK)

            gates(0)
            for i in range(NLAT):
                last = i == NLAT - 1
                with e.Fori(0, PH - 1 if last else PH) as h:
                    e.wait_ge(sem("act_ready"), h + (i * PH + 1))
                    gates(h + (i * PH + 1))
                    diagonals(h + i * PH)
                if last:
                    diagonals(NH - 1)
                for q in range(2):
                    b = full(e, f"acc{i}{q}")
                    a.step(act(accS[:, i, q * 512:(q + 1) * 512], bank(b), ACT.Copy))
                    free(b)
                signal("acc_ready")
            for i in range(NLAT):
                e.wait_ge(sem("fin_sum"), i + 1)
                a.step(act(fsq, accS[:, i, :], ACT.Square, accum_out=stat[:, i:i + 1]))
                a.step(act(stat[:, 8 + i:9 + i], stat[:, i:i + 1], ACT.Sqrt, scale=1.0 / D, bias=eps_c[:, 0:1]))
                signal("fin_std")

        @block.gpsimd
        def _(e):
            e.iota(iota16[:, :], pattern=[[1, 16]], base=0, channel_multiplier=0,
                   allow_small_or_imprecise_dtypes=True).then_inc(sem("iota"), 1)
            e.memset(zmat, 0.0).then_inc(sem("iota"), 1)

            def gather(n, par, ready, idx, copied, ring, slot, table, used):
                e.wait_ge(sem(ready), n + 1)
                if not isinstance(n, int) or n > 0:
                    e.sem_inc(sem("pool_tick"), 1)
                    e.wait_ge(sem(used), n * TOPK - 4)
                    e.sem_inc(sem("pool_tick"), 1)
                e.tensor_copy(idx[:, par, :], idx_all[:, bass.ds(n * 16, 16)]).then_inc(sem(copied), 1)
                e.wait_ge(sem(copied), n + 1)
                e.sem_inc(sem("pool_tick"), 1)
                for s in range(TOPK):
                    if s and s % 4 == 0 and not (isinstance(n, int) and n == 0 and s < 8):
                        e.wait_ge(sem(used), n * TOPK + (s - 4))
                        e.sem_inc(sem("pool_tick"), 1)
                    e.indirect_dma_start(ring[s % 8], None, table,
                                         bass.IndirectOffsetOnAxis(ap=idx[:, par, s:s + 1], axis=0))\
                        .then_inc(sem(f"{slot}{s % 8}"), 16)

            def rows_u(n, par):
                gather(n, par, "idx_ready", idxU, "idxU_copied", Ur, "u_slot", A["peer_u"], "u_used")

            def rows_v(n, par):
                gather(n, par, "idx_ready", idxV, "idxV_copied", Vr, "v_slot", A["peer_v"], "v_used")

            rows_u(0, 0)
            rows_u(1, 1)
            rows_v(0, 0)
            with e.Fori(0, (NH - 2) // 2) as m:
                n = 2 * m + 1
                rows_u(n + 1, 0)
                rows_v(n, 1)
                rows_u(n + 2, 1)
                rows_v(n + 1, 0)
            rows_v(NH - 1, 1)

        @block.vector
        def _(e):
            v = Engine(e, "dve")

            def free(b):
                e.sem_inc(bank_free[b], 1)

            def signal(name):
                e.sem_inc(sem(name), 1)

            tt, ts, stt, cp = e.tensor_tensor, e.tensor_scalar, e.scalar_tensor_tensor, e.tensor_copy
            red = e.tensor_reduce
            nstd = [0]

            def bc(ap, shape):
                return ap.to_broadcast(shape)

            def reciprocal_std(stats):
                nstd[0] += 1
                signal("var_ready")
                e.wait_ge(sem("std_ready"), nstd[0])
                v.step(e.reciprocal(stats[1], stats[1]))

            def layer_norm(x, sq, stats, width, centred=True):
                shape = [P, x.shape[1], width]
                if centred:
                    v.step(red(stats[0], x, AX.X, ALU.add))
                    v.step(ts(stats[0], stats[0], 1.0 / width, None, ALU.mult))
                    v.step(tt(x, x, bc(stats[0].unsqueeze(2), shape), ALU.subtract))
                v.step(tt(sq, x, x, ALU.mult))
                v.step(red(stats[0], sq, AX.X, ALU.add))
                reciprocal_std(stats)
                v.step(tt(x, x, bc(stats[1].unsqueeze(2), shape), ALU.mult))

            for j, val in enumerate((EPS, 1e-12, 64e-5, 1e-5)):
                e.memset(eps_c[:, j:j + 1], val).then_inc(sem("eps"), 1)
            e.wait_ge(sem("csil"), 1)
            for k in range(KT):
                v.do(cp(silA[:, k, 0:64], bc(csil[:, k, 0:1], [P, 64])))
                v.do(cp(silA[:, k, 64:P], bc(csil[:, k, 1:2], [P, 64])))
            v.sync()
            signal("sil_a")
            for g in range(NCTX, NTILE):
                e.wait_ge(sem(f"x{g}"), 32)
                v.step(tt(Xst[g], Xst[g], Pst[g - 2], ALU.add))
                signal("h_sum")
            e.wait_ge(sem("adab"), 16)
            e.wait_ge(sem("x_std"), 1)
            v.step(e.reciprocal(stat[:, 8:8 + NTILE], stat[:, 8:8 + NTILE]))
            for g in range(2):
                v.step(ts(XN[g], Xst[g], stat[:, 8 + g:9 + g], None, ALU.mult))
                signal("xn")
            for n in range(4):
                b = full(e, f"adaA{n}")
                v.step(tt(modA[:, n, :], modA[:, n, :], bank(b), ALU.add))
                free(b)
                signal("mod_a")
            for n in range(4):
                b = full(e, f"mc{n}")
                v.step(cp(modcol[:, 4 * n:4 * n + 4, :], bank(b, 4, 2, 64)[:, :, :, 0]))
                free(b)
            v.step(ts(gcol, modcol[:, 8:16, :], 1.0, None, ALU.add))
            v.step(tt(gcol, gcol, bc(colr("mixg").unsqueeze(2), [P, 8, 2]), ALU.mult))
            signal("gcol")
            for g in range(2, NTILE):
                full(e, f"xt{g - 2}1")
                v.step(ts(XN[g % 2], Xst[g], stat[:, 8 + g:9 + g], None, ALU.mult))
                signal("xn")
            e.wait_ge(sem("h_saved"), 16 * NLAT)
            e.wait_ge(sem("xt_ready"), 2 * NTILE)
            e.wait_ge(sem("levels"), 16)
            v.step(cp(levels[:, :, :], levels_f))
            v.do(e.memset(Apad, 0.0))
            v.do(e.memset(Cp, 0.0))
            v.do(e.memset(Dp, 0.0))
            v.do(e.memset(scanm, 1.0))
            v.sync()
            v.step(e.memset(scanm.rearrange("p (g t) -> p g t", g=NTILE)[:, :, 0:1], 0.0))
            signal("pads")
            e.wait_ge(sem("part_a"), 4)
            v.step(tt(Apad[:, :, 15:15 + SEQ], Araw[:, 0:2, :], Araw[:, 2:4, :], ALU.mult))
            for k in range(TAPS_A):
                for t in range(2):
                    w = cols[:, COLS["acw"][0] + 2 * k + t:COLS["acw"][0] + 2 * k + t + 1]
                    if k == 0:
                        v.do(ts(Ah[:, t, :], Apad[:, t, 0:SEQ], w, col("acb", t), ALU.mult, ALU.add))
                    else:
                        v.e.wait_ge(v.done, v.n - 1)
                        v.do(stt(Ah[:, t, :], Apad[:, t, k:k + SEQ], w, Ah[:, t, :], ALU.mult, ALU.add))
            v.sync()
            signal("a_conv")
            e.wait_ge(sem("params"), 16 * 7)
            b = full(e, "dt")
            v.step(tt(tmp48.rearrange("p (g n) -> p g n", n=8), bank(b)[:, 0:48].rearrange("p (g n) -> p g n", n=8),
                      bc(rows[:, 512:520].unsqueeze(1), [P, NTILE, 8]), ALU.add))
            free(b)
            v.step(stt(tmp48b, tmp48, -1.0, tmp48, ALU.mult, ALU.max))
            signal("dt_abs")
            e.wait_ge(sem("part_c"), 6)
            for t in range(6):
                for k in range(TAPS_C):
                    w = cols[:, COLS["ccw"][0] + 6 * k + t:COLS["ccw"][0] + 6 * k + t + 1]
                    if k:
                        v.sync()
                    for o, i, n in ((0, 0, CTX), (CTX, 260, SEQ)):
                        dst, src = Cx[:, t, o:o + n], Cp[:, t, i + k:i + k + n]
                        if k == 0:
                            v.do(ts(dst, src, w, None, ALU.mult))
                        else:
                            v.do(stt(dst, src, w, dst, ALU.mult, ALU.add))
            v.sync()
            signal("c_taps")
            st4 = (lnst[:, 0, 0:4], lnst[:, 1, 0:4])
            e.wait_ge(sem("a_tok"), 1)
            layer_norm(At, Asq, st4, 256)
            signal("a_norm")
            e.wait_ge(sem("dt_exp"), 1)
            v.step(ts(tmp48b, tmp48b, 1.0, None, ALU.add))
            signal("dt_1p")
            v.step(ts(aneg, aneg, -1.0, None, ALU.mult))
            e.wait_ge(sem("part_v"), 2)
            layer_norm(vt, Bsq, st4, 256)
            v.step(tt(vt, vt, bc(rows[:, 0:256].unsqueeze(1), [P, NLAT, 256]), ALU.mult))
            v.step(tt(vt, vt, bc(rows[:, 256:512].unsqueeze(1), [P, NLAT, 256]), ALU.add))
            signal("b_norm")
            e.wait_ge(sem("dt_ln"), 1)
            v.step(stt(dts, tmp48, 0.0, tmp48b, ALU.max, ALU.add))
            v.step(tt(das.rearrange("p (g n) -> p g n", n=8), dts.rearrange("p (g n) -> p g n", n=8),
                      bc(aneg.unsqueeze(1), [P, NTILE, 8]), ALU.mult))
            signal("c_da")
            dv = lambda x, d: x.rearrange("p (g d h) -> p g d h", d=2, h=HEADS)[:, :, d, :]
            e.wait_ge(sem("c_tok"), 1)
            heads = lambda x: x.rearrange("p g (h e) -> p g h e", h=HEADS)
            for d in range(2):
                v.do(tt(heads(xdt[d]), heads(xs_t)[:, NCTX:], bc(dv(dts, d)[:, NCTX:].unsqueeze(3), [P, NLAT, HEADS, 64]),
                        ALU.mult))
            e.wait_ge(sem("c_dec"), 1)
            for d in range(2):
                v.step(tt(dv(cst, d), dv(dts, d), dv(decs[:, 1 + 2 * d, :], d), ALU.mult))
                v.do(tt(heads(xst[d]), heads(xs_t), bc(dv(cst, d).unsqueeze(3), [P, NTILE, HEADS, 64]), ALU.mult))
            v.sync()
            signal("c_xst")
            for t in range(2):
                b = full(e, f"bm{t}")
                v.step(tt(Bmix[:, t], bank(b, NLAT, P), bc(bsb[:, t, :].unsqueeze(1), [P, NLAT, P]), ALU.add))
                free(b)
                v.step(tt(yT[:, 2 + t, :], Bmix[:, t].rearrange("p a b -> p (a b)"), ut[:, t, :], ALU.mult))
            signal("y_done")

            def decay_rhs(i):
                for d in range(2):
                    if i >= 1:
                        full(e, f"seg{2 * (i - 1) + d}")
                    v.step(tt(seg[d], bc(mat((LE, GE)[d]).unsqueeze(1), [P, HEADS, P]),
                              bc(dv(das, d)[:, NCTX + i, :].unsqueeze(2), [P, HEADS, P]), ALU.mult))
                    signal("c_segrhs")

            def chunk_scores(i):
                b = full(e, f"G{i}")
                for d in range(2):
                    v.do(tt(Gm[d][:, i], bank(b, 2, P), bc(mat((LE, GE)[d]).unsqueeze(1), [P, 2, P]), ALU.mult))
                v.sync()
                free(b)
                if i < NLAT - 1:
                    decay_rhs(i + 1)
                for d in range(2):
                    e.wait_ge(sem("c_L"), 2 * i + d + 1)
                    v.step(tt(Lm[d].rearrange("p (g h) l -> p g h l", g=2), Lm[d].rearrange("p (g h) l -> p g h l", g=2),
                              bc(Gm[d][:, i].unsqueeze(2), [P, 2, 2, P]), ALU.mult))
                    signal("c_M")

            def chunk_outputs(i):
                b = full(e, f"yc{i}")
                y = yC[:, i, :]
                v.step(cp(y, bank(b)[:, 0:256]) if i not in begun else tt(y, y, bank(b)[:, 0:256], ALU.add))
                begun.add(i)
                free(b)

            def chunk_state(step):
                for d in range(2):
                    g = ORDER[d][step]
                    if g >= NCTX:
                        y, new = yC[:, g - NCTX, :], g - NCTX not in begun
                        begun.add(g - NCTX)
                        b = full(e, f"yo{d}{g}")
                        v.step(tt(h64(y if new else Ctmp), h64(bank(b)[:, 0:256]),
                                  bc(dv(decs[:, 2 * d, :], d)[:, g, :].unsqueeze(2), [P, HEADS, 64]), ALU.mult))
                        free(b)
                        if not new:
                            v.step(tt(y, y, Ctmp, ALU.add))
                    if step < NTILE - 1:
                        b = full(e, f"cu{d}{step}")
                        if step == 0:
                            v.step(cp(Sc[d], bank(b)[:, 0:256]))
                        else:
                            v.step(tt(h64(Sc[d]), h64(Sc[d]),
                                      bc(dv(decs[:, 4, :], d)[:, g, :].unsqueeze(2), [P, HEADS, 64]), ALU.mult))
                            v.step(tt(Sc[d], Sc[d], bank(b)[:, 0:256], ALU.add))
                        free(b)
                        signal(f"c_state{d}")

            begun = set()
            h64 = lambda x: x.rearrange("p (h e) -> p h e", h=HEADS)
            decay_rhs(0)
            chunk_scores(0)
            chunk_state(0)
            chunk_state(1)
            for i in range(NLAT):
                chunk_outputs(i)
                if i < NLAT - 1:
                    chunk_scores(i + 1)
                chunk_state(i + 2)
            v.step(tt(heads(Csq), heads(xs_t)[:, NCTX:],
                      bc(rows[:, 528:532].unsqueeze(1).unsqueeze(3), [P, NLAT, HEADS, 64]), ALU.mult))
            v.step(tt(yC, yC, Csq, ALU.add))
            v.step(tt(yC, yC, zt, ALU.mult))
            layer_norm(yC, Csq, st4, 256, centred=False)
            signal("c_norm")
            e.wait_ge(sem("part_d"), 9)
            v.step(tt(mumid, colr("mup"), colr("mun"), ALU.add))
            v.step(ts(mumid, mumid, -1.0, 1.0, ALU.mult, ALU.add))
            for t in range(9):
                for k, w in enumerate((mumid[:, t:t + 1], col("mup", t), col("mun", t))):
                    if k:
                        v.sync()
                    for o, i, n in ((0, 1, CTX), (CTX, 259, SEQ)):
                        sh = (0, -1, 1)[k]
                        dst, src = Dsh[:, t, o:o + n], Dp[:, t, i + sh:i + sh + n]
                        if k == 0:
                            v.do(ts(dst, src, w, None, ALU.mult))
                        else:
                            v.do(stt(dst, src, w, dst, ALU.mult, ALU.add))
            v.sync()
            signal("d_shift")
            r_, k_, v_ = Dsh[:, 0:2, :], Dsh[:, 2:4, :], Dsh[:, 4:6, :]
            full(e, "cb1")
            for t in range(2):
                v.do(ts(kkA[:, t, :], k_[:, t, :], col("kk", t), None, ALU.mult))
            v.step(ts(kam1, colr("ka"), -1.0, 1.0, ALU.mult, ALU.add))
            v.step(tt(Ex, kkA, kkA, ALU.mult))
            signal("d_kksq")
            g6 = lambda x: x.rearrange("p c (g t) -> p c g t", g=NTILE)
            for d in range(2):
                e.wait_ge(sem("d_sw"), d + 1)
                if d == 0:
                    e.wait_ge(sem("d_kkn"), 1)
                    v.step(e.reciprocal(Wx, Wx))
                    v.step(tt(kkA, kkA, Wx, ALU.mult))
                for t in range(2):
                    v.do(e.tensor_tensor_scan(cen[:, t, :], scanm, sw[:, t, :], 0.0, ALU.mult, ALU.add))
                for t in range(2):
                    v.do(ts(kdA[:, t, :], aA[:, t, :], col("ka", t), kam1[:, t:t + 1], ALU.mult, ALU.add))
                v.sync()
                v.do(tt(kdA, kdA, k_, ALU.mult))
                v.do(tt(aA, aA, kkA, ALU.mult))
                v.step(cp(cmid, g6(cen)[:, :, :, 63]))
                for t in range(2):
                    v.do(tt(g6(cen)[:, t], g6(cen)[:, t], bc(cmid[:, t, :].unsqueeze(2), [P, NTILE, P]), ALU.subtract))
                v.sync()
                v.do(tt(Wx, cen, sw, ALU.subtract))
                v.step(cp(kds, kdA[:, :, CTX:]) if d == 0 else tt(kds, kds, kdA[:, :, CTX:], ALU.add))
                signal("d_cen")
                for n in range(3):
                    e.wait_ge(sem("d_ex"), 3 * d + n + 1)
                    if n < 2:
                        for t in range(2):
                            v.do(tt(AR[d][:, t, :, n, :], g6(kkA if n == 0 else r_)[:, t], g6(Ex)[:, t], ALU.mult))
                    else:
                        v.do(tt(Bt[d], aA, Ex, ALU.mult))
                        v.do(tt(Kt[d], kdA, Ex, ALU.mult))
                    v.sync()
                    signal("d_exused")
                signal("d_prep")
                pre, post = (qa, qb) if d == 0 else (qb, qa)
                for r in range(NTILE - 1):
                    v.do(tt(qs[:, d, :, r:r + 1], post[:, d, :, ORDER[d][r]:ORDER[d][r] + 1],
                            pre[:, d, :, ORDER[d][r + 1]:ORDER[d][r + 1] + 1], ALU.mult))
                v.sync()
            f512 = lambda x: x.rearrange("p a b c -> p (a b c)")
            for r in range(NTILE):
                for d in range(2):
                    g = ORDER[d][r]
                    mask = mats[:, (LT, GT)[d]:(LT, GT)[d] + 2, :].rearrange("p a b -> p (a b)")
                    neg = mats[:, (NLT, NGT)[d]:(NLT, NGT)[d] + 2, :].rearrange("p a b -> p (a b)")
                    for hp in range(2):
                        b = full(e, f"kar{r}{d}{hp}")
                        v.step(tt(KAR[d][:, hp], bank(b, 2, 256), bc(mask.unsqueeze(1), [P, 2, 256]), ALU.mult))
                        free(b)
                    for hp in range(2):
                        b = full(e, f"bar{r}{d}{hp}")
                        v.step(tt(BAR[d][:, hp], bank(b, 2, 256), bc(neg.unsqueeze(1), [P, 2, 256]), ALU.mult))
                        free(b)
                    for hp in range(2):
                        b = full(e, f"na{r}{d}{hp}")
                        v.step(tt(NA[d][:, hp], bank(b, 2, P), bc(mat((NGT, NLT)[d]).unsqueeze(1), [P, 2, P]),
                                  ALU.mult))
                        free(b)
                    q4 = lambda x: x.rearrange("p a b c -> p (a b) c")
                    v.do(cp(q4(Xi[d]), bc(mat(IDENT).unsqueeze(1), [P, 4, P])))
                    v.do(cp(q4(Yi[d]), bc(mat(IDENT).unsqueeze(1), [P, 4, P])))
                    v.sync()
                    lx, ly = LEVELS * d, LEVELS * (1 - d)
                    v.do(e.copy_predicated(q4(Xi[d]), bc(levels[:, lx, :].unsqueeze(1), [P, 4, P]), q4(NA[d])))
                    for hp in range(2):
                        v.do(e.copy_predicated(Yi[d][:, hp], bc(levels[:, ly, :].unsqueeze(1), [P, 2, P]),
                                               BAR[d][:, hp, :, 0:P]))
                    v.sync()
                    signal(f"inv{d}")
                for lv in range(1, LEVELS):
                    for d in range(2):
                        lx, ly = LEVELS * d + lv, LEVELS * (1 - d) + lv
                        b2 = full(e, f"PY{r}{d}{lv}")
                        if lv < LEVELS - 1:
                            b1 = full(e, f"PX{r}{d}{lv}")
                            v.do(e.copy_predicated(q4(Xi[d]), bc(levels[:, lx, :].unsqueeze(1), [P, 4, P]),
                                                   bank(b1, 4, P)))
                        v.do(e.copy_predicated(q4(Yi[d]), bc(levels[:, ly, :].unsqueeze(1), [P, 4, P]),
                                               bank(b2, 4, P)))
                        v.sync()
                        if lv < LEVELS - 1:
                            free(b1)
                        free(b2)
                        signal(f"inv{d}")
                for d in range(2):
                    g = ORDER[d][r]
                    b = full(e, f"YU{r}{d}")
                    if r < NTILE - 1:
                        for t in range(2):
                            v.do(stt(T1[d][:, t, :], bank(b)[:, 256 + t * P:256 + (t + 1) * P], qs[:, d, t, r:r + 1],
                                     mat(BLK), ALU.mult, ALU.mult))
                        v.sync()
                        for t in range(2):
                            if r == 0:
                                v.do(cp(Zst[d][:, t, :], T1[d][:, t, :]))
                            else:
                                v.do(stt(Zst[d][:, t, :], Zst[d][:, t, :], qs[:, d, t, r:r + 1], T1[d][:, t, :],
                                         ALU.mult, ALU.add))
                        v.sync()
                        signal(f"d_state{d}")
                    if g >= NCTX:
                        first = (g - NCTX < 2) == (d == 0)
                        y = yD[:, g - NCTX, :]
                        v.step(cp(y, bank(b)[:, 0:256]) if first else tt(y, y, bank(b)[:, 0:256], ALU.add))
                    free(b)
            signal("d_rounds")
            e.wait_ge(sem("d_vt"), 3)
            for k in range(KT):
                v.do(cp(silB[:, k, :], bc(csil[:, k, 0:1], [P, P])))
            v.sync()
            signal("sil_b")
            for t in range(2):
                v.do(stt(rkA[:, t, :], r_[:, t, CTX:], col("rk", t), kds[:, t, :], ALU.mult, ALU.mult))
            v.sync()
            signal("d_rk")
            for t in range(2):
                b = full(e, f"bon{t}")
                v.step(tt(bon[:, t, :], bank(b), v_[:, t, CTX:], ALU.mult))
                free(b)
            layer_norm(yD.rearrange("p i (h e) -> p (i h) e", e=64), Dsq.rearrange("p i (h e) -> p (i h) e", e=64),
                       (lnst[:, 0, :], lnst[:, 1, :]), 64)
            signal("d_gn")
            e.wait_ge(sem("d_gate"), 1)
            e.wait_ge(sem("d_back"), 1)
            v.step(tt(yT[:, 6:8, :], yT[:, 6:8, :], bon, ALU.add))
            v.step(tt(yT[:, 6:8, :], yT[:, 6:8, :], gD, ALU.mult))
            signal("y_done")
            e.wait_ge(sem("adab_b"), 16)
            e.wait_ge(sem("ffn_g"), 16)
            for n in range(8):
                b = full(e, f"adaB{n}")
                v.step(tt(modBn[:, n, :], modBn[:, n, :], bank(b), ALU.add))
                free(b)
            v.step(ts(modB[:, 2, :], modB[:, 2, :], 1.0, None, ALU.add))
            v.step(tt(modB[:, 2, :], modB[:, 2, :], rowG, ALU.mult))
            v.step(cp(gate2, modB[:, 3, :]))
            e.wait_ge(sem("h_load"), 16)
            for i in range(NLAT):
                for q in range(2):
                    sl = slice(q * 512, (q + 1) * 512)
                    b = full(e, f"o{i}{q}")
                    v.step(tt(ytmp, bank(b), modB[:, 0, sl], ALU.mult))
                    free(b)
                    v.step(tt(hL[:, i, sl], hL[:, i, sl], ytmp, ALU.add))
                signal("h2_ready")
            for i in range(NLAT):
                e.wait_ge(sem("f_std"), i + 1)
                v.step(e.reciprocal(stat[:, 8 + i:9 + i], stat[:, 8 + i:9 + i]))
                v.step(stt(f_tok[:, i, :], hL[:, i, :], stat[:, 8 + i:9 + i], modB[:, 2, :], ALU.mult, ALU.mult))
                v.step(tt(f_tok[:, i, :], f_tok[:, i, :], modB[:, 1, :], ALU.add))
                signal("f_ready")
            chain = sem("route_step")
            R = {"n": 0}
            e.wait_ge(sem("iota"), 2)
            NEG = -3.0e38

            def route(n, m):
                k = [0]
                per = 28

                def step(ins):
                    k[0] += 1
                    ins.then_inc(chain, 1)
                    e.wait_ge(chain, m * per + k[0])
                    e.sem_inc(sem("route_tick"), 1)

                sv = s_all.rearrange("p i h a k -> p (i h a k)")
                step(cp(sc[:, :, :].rearrange("p a k -> p (a k)"), sv[:, bass.ds(n * 256, 256)]))
                for half in range(2):
                    step(e.max(v16[:, half, 0:8], sc[:, half, :]))
                    step(e.max_index(i16[:, half, 0:8], v16[:, half, 0:8], sc[:, half, :]))
                    step(e.match_replace(sc2[:, half, :], v16[:, half, 0:8], sc[:, half, :], NEG))
                    step(e.max(v16[:, half, 8:16], sc2[:, half, :]))
                    step(e.max_index(i16[:, half, 8:16], v16[:, half, 8:16], sc2[:, half, :]))
                step(tt(cand.rearrange("p (a b) -> p a b", a=16), bc(v16[:, 0, :].unsqueeze(2), [P, 16, 16]),
                        bc(v16[:, 1, :].unsqueeze(1), [P, 16, 16]), ALU.add))
                step(e.max(top16[:, 0:8], cand))
                step(e.max_index(pos[:, 0:8], top16[:, 0:8], cand))
                step(e.match_replace(cand2, top16[:, 0:8], cand, NEG))
                step(e.max(top16[:, 8:16], cand2))
                step(e.max_index(pos[:, 8:16], top16[:, 8:16], cand2))
                step(ts(posab[:, 0, :], pos[:, :], 4, None, ALU.logical_shift_right))
                step(ts(posab[:, 1, :], pos[:, :], 15, None, ALU.bitwise_and))
                step(cp(posf[:, :, :], posab[:, :, :]))
                step(cp(i16f[:, :, :], i16[:, :, :]))
                for half in range(2):
                    o3 = oh[:, half, :].rearrange("p (a b) -> p a b", a=16)
                    step(tt(o3, bc(posf[:, half, :].unsqueeze(2), [P, 16, 16]),
                            bc(iota16[:, :].unsqueeze(1), [P, 16, 16]), ALU.is_equal))
                    step(tt(o3, o3, bc(i16f[:, half, :].unsqueeze(1), [P, 16, 16]), ALU.mult))
                    step(red(sel[:, half, :], o3, AX.X, ALU.add))
                step(stt(idx_all[:, bass.ds(n * 16, 16)], sel[:, 0, :], float(NKEY), sel[:, 1, :], ALU.mult, ALU.add))
                ts(top_all[:, bass.ds(n * 16, 16)], top16[:, :], top16[:, 0:1], None, ALU.subtract)\
                    .then_inc(sem("idx_ready"), 1)
                assert k[0] == per, k[0]

            def dot_products(n, i):
                for s in range(TOPK):
                    e.wait_ge(sem(f"u_slot{s % 8}"), n * 32 + 16 * (s // 8 + 1))
                    e.tensor_tensor_reduce(Ur[s % 8], Ur[s % 8], f_tok[:, i, :], 1.0, 0.0, ALU.mult, ALU.add,
                                           dots[:, s:s + 1]).then_inc(sem("u_used"), 1)

            def weights(n):
                e.wait_ge(sem("gates"), n * 2 + 2)
                e.reciprocal(esum[:, 1:2], esum[:, 0:1]).then_inc(sem("inverse_sum"), 1)
                e.wait_ge(sem("inverse_sum"), n + 1)
                stt(act_all[:, bass.ds(n * 16, 16)], gel[:, :], esum[:, 1:2], egate[:, :], ALU.mult, ALU.mult)\
                    .then_inc(sem("act_ready"), 1)

            e.wait_ge(sem("s_ready"), 4)
            route(0, 0)
            route(1, 1)
            for i in range(NLAT):
                last = i == NLAT - 1
                if not last:
                    e.wait_ge(sem("s_ready"), 4 * (i + 2))
                with e.Fori(0, PH - 2 if last else PH) as h:
                    n = h + i * PH
                    dot_products(n, i)
                    route(n + 2, n + 2)
                    weights(n)
                if last:
                    for n in (NH - 2, NH - 1):
                        dot_products(n, i)
                        weights(n)
            e.wait_ge(sem("hfin"), 32)
            for i in range(NLAT):
                e.wait_ge(sem("acc_ready"), i + 1)
                v.step(tt(accS[:, i, :], accS[:, i, :], gate2, ALU.mult))
                v.step(tt(accS[:, i, :], accS[:, i, :], hfin[:, i, :], ALU.add))
                signal("fin_sum")
                e.wait_ge(sem("fin_std"), i + 1)
                v.step(e.reciprocal(stat[:, 8 + i:9 + i], stat[:, 8 + i:9 + i]))
                v.step(stt(hfin[:, i, :], accS[:, i, :], stat[:, 8 + i:9 + i], rowF, ALU.mult, ALU.mult))
                signal("out_tile")


def positions():
    grid_w = 64
    row = np.repeat(np.arange(SEQ // grid_w), grid_w).astype(np.float32)
    column = np.tile(np.arange(grid_w), SEQ // grid_w).astype(np.float32)
    q = D // 4
    freq = (10000.0 ** (-np.arange(q, dtype=np.float64) / q)).astype(np.float32)
    ar, ac = row[:, None] * freq, column[:, None] * freq
    return np.concatenate([np.sin(ar), np.cos(ar), np.sin(ac), np.cos(ac)], -1).astype(np.float32)


def constant_matrices():
    p, f = np.arange(P)[:, None], np.arange(P)[None, :]
    one = lambda c: c.astype(np.float32)
    m = [one(p == f), one(p < f), one(p <= f), one(p > f), one(p >= f),
         -one(p < f), -one(p <= f), -one(p > f), -one(p >= f), one(p >= 0) * one(f >= 0), one(p // 64 == f // 64)]
    lower = [((p >> (n + 1)) == (f >> (n + 1))) & ((p >> n) & 1 == 1) & ((f >> n) & 1 == 0) for n in range(LEVELS)]
    lv = np.stack(lower + [x.T for x in lower]).astype(np.float32)
    return np.ascontiguousarray(np.stack(m).transpose(1, 0, 2)), np.ascontiguousarray(lv.transpose(1, 0, 2))


def kernel(**inputs):
    import concourse.bacc as bacc
    from concourse.bass_utils import run_bass_kernel_spmd

    g = {k: np.asarray(v) for k, v in inputs.items()}

    def columns(a):
        return np.reshape(a, (-1, P)).T

    def over_partitions(a):
        return np.broadcast_to(np.reshape(a, (1,) + a.shape), (P,) + a.shape)

    w_in = g["w_in"][0]
    mats, levels = constant_matrices()
    ada_w = g["ada_w"][0].reshape(KT, P, 12, 512).transpose(2, 1, 0, 3)
    ada_b = g["ada_b"][0].reshape(12, 512)
    arrays = {
        "x": g["x"][0], "ctx": g["ctx"][0], "pos": positions(), "mats": mats, "levels": levels,
        "cc": np.stack([g["c"][0], g["c_ctx"]]).reshape(2, KT, P).transpose(2, 1, 0),
        "ada_w": ada_w, "adab_a": over_partitions(ada_b[0:4]), "adab_b": over_partitions(ada_b[4:12]),
        "cols": np.concatenate([columns(a) for a in (
            g["norm_mix_g"], g["a_conv_w"], g["a_conv_b"], g["a_ln_g"], g["a_ln_b"], g["c_conv_w"], g["c_conv_b"],
            g["d_mu_prev"], g["d_mu_next"], g["d_w0"], g["d_a0"], g["d_k_k"], g["d_k_a"], g["d_r_k"],
            g["d_gn_g"], g["d_gn_b"], g["c_norm_g"])], axis=1),
        "rows": over_partitions(np.concatenate([g["b_ln_g"][0], g["b_ln_b"][0], g["c_dt_bias"][0].reshape(-1),
                                                g["c_a_log"][0].reshape(-1), g["c_d"][0]])),
        "bsb": np.repeat(g["b_bs"][0], 64, axis=0).reshape(2, P, P).transpose(1, 0, 2),
        "wsT": g["b_ws"][0].transpose(2, 0, 1),
        "wdt": w_in[:, OFF_D - 8:OFF_D].reshape(KT, P, 8).transpose(1, 0, 2),
        "w2": g["d_w2"][0].reshape(P, 256), "a2": g["d_a2"][0].reshape(P, 256), "g2": g["d_g2"][0],
        "w_in": np.stack([w_in[:, c:c + P].reshape(KT, P, P).transpose(1, 0, 2) for c, _ in COL_TILES]),
        "w_out": g["w_out"][0].reshape(KT, P, D).transpose(1, 0, 2),
        "wqT": g["peer_wq"][0].T.reshape(16, P, D), "k1T": g["peer_k1"][0].T, "k2T": g["peer_k2"][0].T,
        "ffn_g": over_partitions(g["norm_ffn_g"][0]), "fin_g": over_partitions(g["final_g"]),
        "peer_u": g["peer_u"][0], "peer_v": g["peer_v"][0],
    }
    nc = bacc.Bacc("TRN2", target_bir_lowering=False, num_devices=1)
    in_map, aps = {}, {}
    for name, a in arrays.items():
        a = np.ascontiguousarray(a)
        in_map[f"in_{name}"] = a
        aps[name] = nc.dram_tensor(f"in_{name}", a.shape, mybir.dt.from_np(a.dtype), kind="ExternalInput").ap()
    out = nc.dram_tensor("out_0", (SEQ, D), F32, kind="ExternalOutput").ap()
    build_program(nc, aps, out)
    r = run_bass_kernel_spmd(nc, [in_map], core_ids=[0])
    return np.reshape(r.results[0]["out_0"], (1, SEQ, D))
```

```python
from contextlib import ExitStack

import numpy as np
import concourse.bass as bass
from concourse import mybir

F32 = mybir.dt.float32
U32 = mybir.dt.uint32
U8 = mybir.dt.uint8
ALU = mybir.AluOpType
ACT = mybir.ActivationFunctionType
AX = mybir.AxisListType

P = 128
D = 1024
KT = D // P
SEQ, CTX = 512, 256
NLAT, NCTX = SEQ // P, CTX // P
NTILE = NLAT + NCTX
TOK = SEQ + CTX
EPS = 1e-6
OFF_B, OFF_C, OFF_D = 512, 1024, 2056
TAPS_A, TAPS_C = 31, 5
HEADS = 4
LOGW = float(np.exp(-0.5))
PH, TOPK, NKEY, NEXP = 8, 16, 128, 16384
HEAD_PARTS = ((0, 1), (1, 2), (2, 3), (3, 4), (4, PH))
LEVELS = 7

COL_TILES = ([(128 * j, "a") for j in range(4)] + [(OFF_B + 128 * j, "u") for j in range(2)]
             + [(OFF_B + 256 + 128 * j, "v") for j in range(2)]
             + [(OFF_C + 256 + 128 * j, "c") for j in range(6)]
             + [(OFF_C + 128 * j, "z") for j in range(2)]
             + [(OFF_D + 128 * j, "d") for j in range(9)])
DT_AFTER = 13

BETWEEN = {(14, 0): ["a_tok"], (15, 0): ["dt_exp"], (16, 1): ["c_silu"], (17, 0): ["c_tok", "a_std"],
           (18, 0): ["a_back", "b_std"], (18, 1): ["c_decay"], (19, 0): ["b_mix"], (19, 1): ["G0", "state0"],
           (20, 0): ["state1"], (20, 1): ["Y0", "G1"], (21, 0): ["state2"], (21, 1): ["Y1", "G2"],
           (22, 0): ["state3"], (22, 1): ["Y2", "G3"], (23, 0): ["state4"], (23, 1): ["Y3"], (24, 0): ["state5"]}

ADA_HALVES = []
_last = {}
_count = {"ada_slot0": 32, "ada_slot1": 32, "w_slot3": 96, "x4": 32, "x5": 32}
_area_sem = {119: "ada_slot0", 111: "ada_slot1", 103: "w_slot3", 95: "x4", 87: "x5", 159: "w_slot3", 167: "x5"}
for _m, _kb in enumerate((119, 111, 103, 95, 87, 119, 111, 95) + (159, 167) * 4):
    _count[_area_sem[_kb]] += 16
    ADA_HALVES.append((_kb, _last.get(_kb), _area_sem[_kb], _count[_area_sem[_kb]]))
    _last[_kb] = _m

COLS = {}
_n = 0
for _name, _c in (("mixg", 8), ("acw", 62), ("acb", 2), ("alg", 2), ("alb", 2), ("ccw", 30), ("ccb", 6),
                  ("mup", 9), ("mun", 9), ("w0", 4), ("a0", 4), ("kk", 2), ("ka", 2), ("rk", 2),
                  ("gng", 2), ("gnb", 2), ("cng", 2)):
    COLS[_name] = (_n, _c)
    _n += _c
NCOL = _n
ROWS = {"blg": (0, 256), "blb": (256, 256), "dtb": (512, 8), "alog": (520, 8), "cd": (528, 4)}
NROW = 532

IDENT, LT, LE, GT, GE, NLT, NLE, NGT, NGE, ONES, BLK, KEY1, KEY2 = range(13)
NMAT = 11


def build_program(nc, A, out):
    ctx = ExitStack()
    with ctx:
        sem_cache = {}

        def sem(name):
            if name not in sem_cache:
                sem_cache[name] = ctx.enter_context(nc.semaphore(name))
            return sem_cache[name]

        arena = ctx.enter_context(nc.sbuf_tensor("arena", [P, 200 * 256], F32))
        levels = ctx.enter_context(nc.sbuf_tensor("levels", [P, 2 * LEVELS, P], U8))
        psum = ctx.enter_context(nc.psum_tensor("psum", [P, 8 * 512], F32))
        h_dram = nc.dram_tensor("h_scratch", (SEQ, D), F32, kind="Internal").ap()
        mod_dram = nc.dram_tensor("mod_scratch", (1, 8 * 512), F32, kind="Internal").ap()
        h2_dram = nc.dram_tensor("h2_scratch", (SEQ, D), F32, kind="Internal").ap()

        def at(kb, *shape):
            n = int(np.prod(shape))
            v = arena[:, int(kb * 256):int(kb * 256) + n]
            names = "abcd"[:len(shape)]
            if len(shape) == 1:
                return v
            return v.rearrange(f"p ({' '.join(names)}) -> p {' '.join(names)}",
                               **{k: s for k, s in zip(names, shape)})

        def bank(b, *shape):
            n = int(np.prod(shape)) if shape else 512
            v = psum[:, b * 512:b * 512 + n]
            if len(shape) < 2:
                return v
            names = "abcd"[:len(shape)]
            return v.rearrange(f"p ({' '.join(names)}) -> p {' '.join(names)}",
                               **{k: s for k, s in zip(names, shape)})

        mats = at(0, 14, P)
        mat = lambda i: mats[:, i, :]
        scanm = at(9, TOK)
        cols = at(12, NCOL)
        col = lambda name, j=0: cols[:, COLS[name][0] + j:COLS[name][0] + j + 1]
        colr = lambda name: cols[:, COLS[name][0]:COLS[name][0] + COLS[name][1]]
        yT = at(13, 8, SEQ)
        small = at(29, 768)
        csil = small[:, 0:16].rearrange("p (k s) -> p k s", s=2)
        modcol = small[:, 16:48].rearrange("p (k s) -> p k s", s=2)
        gcol = small[:, 48:64].rearrange("p (k s) -> p k s", s=2)
        stat = small[:, 64:80]
        eps_c = small[:, 80:84]
        kam1 = small[:, 84:86]
        cmid = small[:, 720:732].rearrange("p (c g) -> p c g", c=2)
        mumid = small[:, 86:95]
        dts = small[:, 96:144]
        das = small[:, 144:192]
        tmp48 = small[:, 192:240]
        decs = small[:, 240:480].rearrange("p (m n) -> p m n", m=5)
        cst = small[:, 480:528]
        aneg = small[:, 528:536]
        qa = small[:, 536:560].rearrange("p (d c g) -> p d c g", d=2, c=2)
        qb = small[:, 560:584].rearrange("p (d c g) -> p d c g", d=2, c=2)
        qs = small[:, 584:608].rearrange("p (d c g) -> p d c g", d=2, c=2)
        lnst = small[:, 608:672].rearrange("p (a b) -> p a b", a=4)
        tmp48b = small[:, 672:720]

        Dp = at(32, 9, 772)
        Dsh = at(60, 9, TOK)
        Xst = [at(k, D) for k in (48, 52, 56, 60, 64, 68)]
        Pst = [at(k, D) for k in (72, 76, 80, 154)]
        XN = [at(179 + 4 * i, D) for i in range(2)]
        sqs = at(158, D)
        levels_f = at(163, 2 * LEVELS, P)
        adaA = [at(32, KT, 512), at(127, KT, 512)]
        silA = at(146, KT, P)
        modA = at(171, 4, 512)
        XT = at(87, KT, TOK)
        wring = [at(111 + 4 * i, KT, P) for i in range(4)]
        Cp = at(127, 6, 776)
        Araw = at(146, 4, SEQ)
        zt = at(154, NLAT, 256)
        vt = at(158, NLAT, 256)
        ut = at(162, 2, SEQ)
        Apad = at(166, 2, 542)
        Cx = at(171, 6, TOK)
        rows = at(189, NROW)
        bsb = at(191.5, 2, P)
        wsT = at(192.5, HEADS, P)
        wdt = at(194.5, KT, 8)
        w2s = at(195, 256)
        a2s = at(196, 256)
        g2s = at(197, 256)
        Ah = at(146, 2, SEQ)
        At = at(150, NLAT, 256)
        Asq = at(166, NLAT, 256)
        Bsq = at(166, NLAT, 256)
        Bmix = at(139, 2, NLAT, P)
        xs_t = at(60, NTILE, 256)
        B_t = at(66, NTILE, 256)
        xdt = [at(72 + 4 * d, NLAT, 256) for d in range(2)]
        Lm = [at(80 + 2 * i, HEADS, P) for i in range(2)]
        Sc = [at(84 + d, 256) for d in range(2)]
        Ctmp = at(86, 256)
        xst = [at(127 + 6 * d, NTILE, 256) for d in range(2)]
        seg = [at(139 + 2 * i, HEADS, P) for i in range(2)]
        Gm = [at(146 + 4 * d, NLAT, 2, P) for d in range(2)]
        Csq = at(158, NLAT, 256)
        yC = at(166, NLAT, 256)
        sw = at(32, 2, TOK)
        cen = at(38, 2, TOK)
        Wx = at(44, 2, TOK)
        Ex = at(50, 2, TOK)
        kds = at(56, 2, SEQ)
        aA = at(87, 2, TOK)
        kdA = at(99, 2, TOK)
        kkA = at(105, 2, TOK)
        AR = [at(111 + 12 * d, 2, NTILE, 2, P) for d in range(2)]
        Bt = [at(135 + 6 * d, 2, TOK) for d in range(2)]
        Kt = [at(147 + 6 * d, 2, TOK) for d in range(2)]
        base = (159, 87)
        KAR = [at(base[d], 2, 2, 256) for d in range(2)]
        BAR = [at(base[d] + 4, 2, 2, 256) for d in range(2)]
        NA = [at(base[d] + 8, 2, 2, P) for d in range(2)]
        Xi = [at(base[d] + 10, 2, 2, P) for d in range(2)]
        Yi = [at(base[d] + 12, 2, 2, P) for d in range(2)]
        Ri = [at(base[d] + 14, 2, 2, P) for d in range(2)]
        Vt = at(175, NTILE, 256)
        KB = [at(181 + 2 * d, 2, 256) for d in range(2)]
        Zs = [at(103 + d, 256) for d in range(2)]
        SAs = [at(105 + d, 256) for d in range(2)]
        Zst = [at(107 + d, 2, P) for d in range(2)]
        T1 = [at(109 + d, 2, P) for d in range(2)]
        yD = at(32, NLAT, 256)
        gD = at(116, 2, SEQ)
        bon = at(120, 2, SEQ)
        Dsq = at(100, NLAT, 256)
        rkA = at(190, 2, SEQ)
        w_o = at(32, KT, D)
        hL = at(64, NLAT, D)
        zrhs = at(0, 512)
        modBn = at(80, 8, 512)
        modB = at(80, 4, D)
        rowG = at(96, D)
        f_tok = at(104, NLAT, D)
        fT = at(120, KT, P)
        wqr = [at(104 + 4 * i, D) for i in range(3)]
        adaB = [at(kb, 4, 512) for kb, _, _, _ in ADA_HALVES]
        mod_row = [at(185 + 2 * i, 512) for i in range(2)]
        Wp = at(124, KT, 2048)
        ytmp = at(188, 512)
        osq = at(190, D)
        s_all = at(64, NLAT, PH, 2, P)
        Ur = [at(32 + 4 * i, D) for i in range(8)]
        Vr = [at(k, D) for k in (13, 17, 21, 25, 188, 192, 196, 100)]
        gate2 = at(96, D)
        accS = at(64, NLAT, 2, D)[:, :, 0, :]
        hfin = at(140, NLAT, D)
        rowF = at(156, D)
        fsq = at(160, D)

        def own(name, shape, dt=F32):
            return ctx.enter_context(nc.sbuf_tensor(name, shape, dt))

        NH = NLAT * PH
        iota16 = own("iota16", [P, 16])
        dots = own("dots", [P, 16])
        gel = own("gel", [P, 16])
        egate = own("egate", [P, 16])
        esum = own("esum", [P, 2])
        act_cur = own("act_cur", [P, 16])
        zmat_t = own("zmat", [P, P])
        zmat = zmat_t[:, :]
        diag = at(7, 2, P)
        idx_all = own("idx_all", [P, NH * 16], U32)
        act_all = at(9, NH * 16)
        top_all = at(11, NH * 16)
        idxU = own("idxU", [P, 2, 16], U32)
        idxV = own("idxV", [P, 2, 16], U32)
        sc = at(8, 2, P)
        sc2 = at(31, 2, P)
        v16 = own("v16", [P, 2, 16])
        i16 = own("i16", [P, 2, 16], U32)
        i16f = own("i16f", [P, 2, 16])
        cand = at(5, 256)
        cand2 = at(6, 256)
        oh = at(3, 2, 256)
        top16 = own("top16", [P, 16])
        pos = own("pos", [P, 16], U32)
        posab = own("posab", [P, 2, 16], U32)
        posf = own("posf", [P, 2, 16])
        sel = own("sel", [P, 2, 16])

        class Engine:

            def __init__(self, eng, name):
                self.e, self.n, self.done = eng, 0, sem(f"{name}_done")

            def do(self, ins):
                self.n += 1
                ins.then_inc(self.done, 1)

            def sync(self):
                self.e.wait_ge(self.done, self.n)

            def step(self, ins):
                self.do(ins)
                self.sync()

        bank_full = [sem(f"bank_full{b}") for b in range(8)]
        bank_free = [sem(f"bank_free{b}") for b in range(8)]
        uses, owed, use_of = [0] * 8, [0] * 8, {}
        freed = [0] * 8

        def take(pe, name, b, readers=1):
            if owed[b]:
                pe.wait_ge(bank_free[b], owed[b])
            uses[b] += 1
            owed[b] += readers
            use_of[name] = (b, uses[b])
            return b

        def full(e, name):
            b, k = use_of[name]
            e.wait_ge(bank_full[b], k)
            return b

        def give(ins, b):
            ins.then_inc(bank_full[b], 1)

        block = ctx.enter_context(nc.Block())
        ORDER = [[0, 1, 2, 3, 4, 5], [1, 0, 5, 4, 3, 2]]
        fL = float(P)

        @block.tensor
        def _(pe):
            def mm(o, l, r, start=True, stop=True, **k):
                return pe.matmul(o, l, r, start=start, stop=stop, **k)

            def tr(o, i):
                return pe.transpose(o, i, mat(IDENT))

            pe.wait_ge(sem("consts"), 16)
            pe.wait_ge(sem("iota"), 2)
            pe.wait_ge(sem("sil_a"), 1)
            for n in range(4):
                b = take(pe, f"adaA{n}", n % 2)
                pe.wait_ge(sem(f"ada_slot{n % 2}"), 16 * (n // 2 + 1))
                for k in range(KT):
                    last = mm(bank(b), silA[:, k, :], adaA[n % 2][:, k, :], k == 0, k == KT - 1)
                give(last, b)
            for n in range(4):
                b = take(pe, f"mc{n}", 2 + n)
                pe.wait_ge(sem("mod_a"), n + 1)
                for j in range(4):
                    last = tr(bank(b)[:, j * P:(j + 1) * P], modA[:, n, j * P:(j + 1) * P])
                give(last, b)
            for g in range(NTILE):
                pe.wait_ge(sem("xn"), g + 1)
                for q in range(2):
                    b = take(pe, f"xt{g}{q}", (2 * g + q) % 8)
                    for j in range(4):
                        k = 4 * q + j
                        last = tr(bank(b)[:, j * P:(j + 1) * P], XN[g % 2][:, k * P:(k + 1) * P])
                    give(last, b)

            def a_tok():
                pe.wait_ge(sem("a_conv"), 1)
                for t in range(2):
                    b = take(pe, f"at{t}", 5 + t)
                    for i in range(NLAT):
                        last = tr(bank(b)[:, i * P:(i + 1) * P], Ah[:, t, i * P:(i + 1) * P])
                    give(last, b)

            def a_back():
                pe.wait_ge(sem("a_norm"), 1)
                for t in range(2):
                    b = take(pe, f"ab{t}", 6 + t)
                    for i in range(NLAT):
                        last = tr(bank(b)[:, i * P:(i + 1) * P], At[:, i, t * P:(t + 1) * P])
                    give(last, b)

            def b_mix():
                pe.wait_ge(sem("b_norm"), 1)
                for t in range(2):
                    b = take(pe, f"bm{t}", 4 + t)
                    for i in range(NLAT):
                        for hp in range(2):
                            h = 2 * t + hp
                            last = mm(bank(b)[64 * hp:64 * hp + 64, i * P:(i + 1) * P],
                                      vt[:, i, h * 64:(h + 1) * 64], wsT[:, h, :])
                    give(last, b)

            def c_tok():
                pe.wait_ge(sem("c_conv"), 1)
                for t in range(4):
                    for q in range(2):
                        b = take(pe, f"ct{t}{q}", 4 + (2 * t + q) % 4)
                        for gg in range(3):
                            g = 3 * q + gg
                            last = tr(bank(b)[:, gg * P:(gg + 1) * P], Cx[:, t, g * P:(g + 1) * P])
                        give(last, b)

            def c_decay():
                pe.wait_ge(sem("c_da"), 1)
                b = take(pe, "dec", 6)
                for m, which in enumerate((LE, GT, GE, LT, ONES)):
                    last = mm(bank(b)[:, m * 48:(m + 1) * 48], mat(which), das)
                give(last, b)

            def chunk_scores(i):
                b = take(pe, f"G{i}", 4 + i % 2)
                sl = slice(CTX + i * P, CTX + (i + 1) * P)
                for gr in range(2):
                    last = mm(bank(b)[:, gr * P:(gr + 1) * P], Cx[:, 2 + gr, sl], Cx[:, 4 + gr, sl])
                give(last, b)
                for d in range(2):
                    n = 2 * i + d
                    pe.wait_ge(sem("c_segrhs"), n + 1)
                    b = take(pe, f"seg{n}", 6 + d)
                    give(mm(bank(b), mat((GT, LT)[d]), seg[d].rearrange("p a b -> p (a b)")), b)

            def chunk_outputs(i):
                b = take(pe, f"yc{i}", 4 + i % 2)
                pe.wait_ge(sem("c_M"), 2 * i + 2)
                for h in range(HEADS):
                    for d in range(2):
                        last = mm(bank(b)[:, h * 64:(h + 1) * 64], Lm[d][:, h, :],
                                  xdt[d][:, i, h * 64:(h + 1) * 64], d == 0, d == 1)
                give(last, b)

            def chunk_state(step):
                for d in range(2):
                    g = ORDER[d][step]
                    if g >= NCTX:
                        pe.wait_ge(sem(f"c_state{d}"), step)
                        b = take(pe, f"yo{d}{g}", 4 + d)
                        for gr in range(2):
                            last = mm(bank(b)[:, gr * P:(gr + 1) * P], Cx[:, 4 + gr, g * P:(g + 1) * P],
                                      Sc[d][:, gr * P:(gr + 1) * P])
                        give(last, b)
                    if step < NTILE - 1:
                        if step == 0:
                            pe.wait_ge(sem("c_xst"), 1)
                        b = take(pe, f"cu{d}{step}", 6 + d)
                        for gr in range(2):
                            last = mm(bank(b)[:, gr * P:(gr + 1) * P], B_t[:, g, gr * P:(gr + 1) * P],
                                      xst[d][:, g, gr * P:(gr + 1) * P])
                        give(last, b)

            def between(j, part):
                for name in BETWEEN.get((j, part), ()):
                    if name == "a_tok":
                        a_tok()
                    elif name == "a_back":
                        a_back()
                    elif name == "b_mix":
                        b_mix()
                    elif name == "c_tok":
                        c_tok()
                    elif name == "c_decay":
                        c_decay()
                    elif name[0] == "G":
                        chunk_scores(int(name[1]))
                    elif name[0] == "Y":
                        chunk_outputs(int(name[1]))
                    elif name[:5] == "state":
                        chunk_state(int(name[5]))

            pe.wait_ge(sem("xt_ready"), 2 * NTILE)
            pe.wait_ge(sem("params"), 16 * 7)
            for j, (_, part) in enumerate(COL_TILES):
                w = wring[j % 4]
                pe.wait_ge(sem(f"w_slot{j % 4}"), 16 * (j // 4 + 1))
                b = take(pe, f"p{j}", j % 2)
                if part in "zv":
                    for i in range(NLAT):
                        for k in range(KT):
                            last = mm(bank(b)[:, i * P:(i + 1) * P], XT[:, k, CTX + i * P:CTX + (i + 1) * P],
                                      w[:, k, :], k == 0, k == KT - 1)
                else:
                    for k in range(KT):
                        last = mm(bank(b), w[:, k, :], XT[:, k, CTX:], k == 0, k == KT - 1)
                give(last, b)
                between(j, 0)
                if part in "cd":
                    b = take(pe, f"pc{j}", 2 + j % 2)
                    for k in range(KT):
                        last = mm(bank(b)[:, 0:CTX], w[:, k, :], XT[:, k, 0:CTX], k == 0, k == KT - 1)
                    give(last, b)
                    between(j, 1)
                if j == DT_AFTER:
                    b = take(pe, "dt", 4)
                    for g in range(NTILE):
                        for k in range(KT):
                            last = mm(bank(b)[:, g * 8:g * 8 + 8], XT[:, k, g * P:(g + 1) * P], wdt[:, k, :],
                                      k == 0, k == KT - 1)
                    give(last, b)

            def adaln_row(n):
                b = take(pe, f"adaB{n}", 6 + n % 2)
                for q in range(2):
                    _, _, loaded, count = ADA_HALVES[2 * n + q]
                    pe.wait_ge(sem(loaded), count)
                    for k in range(4):
                        last = mm(bank(b)[0:1, :], csil[:, 4 * q + k, 0:1], adaB[2 * n + q][:, k, :],
                                  q + k == 0, False)
                    last.then_inc(sem("adaB_used"), 1)
                pe.wait_ge(sem(f"adaB_bias{n % 2}"), 16 * (n // 2 + 1))
                give(mm(bank(b)[0:1, :], mat(ONES)[0:1, 0:1], mod_row[n % 2][0:1, :], False, True), b)

            for n in range(3):
                adaln_row(n)
            pe.wait_ge(sem("c_norm"), 1)
            for t in range(2):
                b = take(pe, f"cb{t}", 6 + t)
                for i in range(NLAT):
                    last = tr(bank(b)[:, i * P:(i + 1) * P], yC[:, i, t * P:(t + 1) * P])
                give(last, b)
            adaln_row(3)
            pe.wait_ge(sem("d_tanh"), 1)
            n = 0
            for d in range(2):
                for kind, wt, src in (("w", w2s, 6), ("a", a2s, 7)):
                    for t in range(2):
                        b0 = 2 * (n % (4 - d))
                        b1 = b0 + 1
                        take(pe, f"l{kind}{d}{t}", b0)
                        give(mm(bank(b0), wt[64 * d:64 * d + 64, t * P:(t + 1) * P],
                                Dsh[64 * d:64 * d + 64, src, CTX:]), b0)
                        take(pe, f"lc{kind}{d}{t}", b1)
                        give(mm(bank(b1)[:, 0:CTX], wt[64 * d:64 * d + 64, t * P:(t + 1) * P],
                                Dsh[64 * d:64 * d + 64, src, 0:CTX]), b1)
                        n += 1
                if d == 0:
                    pe.wait_ge(sem("d_kksq"), 1)
                    for t in range(2):
                        b0, b1 = 2 * (n % 4), 2 * (n % 4) + 1
                        take(pe, f"kn{t}", b0)
                        give(mm(bank(b0), mat(BLK), Ex[:, t, CTX:]), b0)
                        take(pe, f"knc{t}", b1)
                        give(mm(bank(b1)[:, 0:CTX], mat(BLK), Ex[:, t, 0:CTX]), b1)
                        n += 1
                    for row in range(4, 7):
                        adaln_row(row)
            adaln_row(7)
            for g in range(NTILE):
                if g % 2 == 0:
                    b = take(pe, f"vt{g // 2}", 2 * (g // 2))
                for t in range(2):
                    o = ((g % 2) * 2 + t) * P
                    last = tr(bank(b)[:, o:o + P], Dsh[:, 4 + t, g * P:(g + 1) * P])
                if g % 2:
                    give(last, b)
            pe.wait_ge(sem("d_prep"), 2)
            for r in range(NTILE):
                for d in range(2):
                    g = ORDER[d][r]
                    tk = slice(g * P, (g + 1) * P)
                    for hp in range(2):
                        hs = slice(64 * hp, 64 * hp + 64)
                        take(pe, f"kar{r}{d}{hp}", hp)
                        for t in range(2):
                            last = mm(bank(hp)[:, t * 256:(t + 1) * 256], Kt[d][hs, t, tk],
                                      AR[d][hs, t, g, :, :].rearrange("p a b -> p (a b)"))
                        give(last, hp)
                    for hp in range(2):
                        hs = slice(64 * hp, 64 * hp + 64)
                        take(pe, f"bar{r}{d}{hp}", 2 + hp)
                        for t in range(2):
                            last = mm(bank(2 + hp)[:, t * 256:(t + 1) * 256], Bt[d][hs, t, tk],
                                      AR[d][hs, t, g, :, :].rearrange("p a b -> p (a b)"))
                        give(last, 2 + hp)
                    for hp in range(2):
                        hs = slice(64 * hp, 64 * hp + 64)
                        take(pe, f"na{r}{d}{hp}", 4 + hp)
                        for t in range(2):
                            last = mm(bank(4 + hp)[:, t * P:(t + 1) * P], AR[d][hs, t, g, 0, :], Bt[d][hs, t, tk])
                        give(last, 4 + hp)
                    b = take(pe, f"kbt{r}{d}", 6 + d)
                    for t in range(2):
                        tr(bank(b)[:, t * P:(t + 1) * P], Kt[d][:, t, tk])
                    for t in range(2):
                        last = tr(bank(b)[:, (2 + t) * P:(3 + t) * P], Bt[d][:, t, tk])
                    give(last, b)
                for lv in range(1, LEVELS):
                    for d in range(2):
                        pe.wait_ge(sem(f"inv{d}"), LEVELS * r + lv)
                        b = take(pe, f"R{r}{d}{lv}", 3 * d)
                        for q in range(4):
                            last = mm(bank(b)[:, q * P:(q + 1) * P], NA[d][:, q // 2, q % 2, :],
                                      Yi[d][:, q // 2, q % 2, :])
                        give(last, b)
                    for d in range(2):
                        pe.wait_ge(sem(f"invR{d}"), (LEVELS - 1) * r + lv)
                        if lv < LEVELS - 1:
                            b = take(pe, f"PX{r}{d}{lv}", 3 * d + 1)
                            for q in range(4):
                                last = mm(bank(b)[:, q * P:(q + 1) * P], Ri[d][:, q // 2, q % 2, :],
                                          Xi[d][:, q // 2, q % 2, :])
                            give(last, b)
                        b = take(pe, f"PY{r}{d}{lv}", 3 * d + 2)
                        for q in range(4):
                            last = mm(bank(b)[:, q * P:(q + 1) * P], Xi[d][:, q // 2, q % 2, :],
                                      Ri[d][:, q // 2, q % 2, :])
                        give(last, b)
                for d in range(2):
                    g = ORDER[d][r]
                    tk = slice(g * P, (g + 1) * P)
                    b = take(pe, f"Z{r}{d}", 6 + d)
                    if r > 0:
                        pe.wait_ge(sem(f"d_state{d}"), r)
                    pe.wait_ge(sem("d_vt"), 3)
                    for t in range(2):
                        if r > 0:
                            mm(bank(b)[:, t * P:(t + 1) * P], AR[d][:, t, g, 0, :], Zst[d][:, t, :], True, False,
                               skip_group_check=True)
                        for hp in range(2):
                            h = 2 * t + hp
                            last = mm(bank(b)[:, h * 64:(h + 1) * 64], KAR[d][:, hp, t, 0:P],
                                      Vt[:, g, h * 64:(h + 1) * 64], r == 0, True, skip_group_check=r > 0)
                    give(last, b)
                for d in range(2):
                    pe.wait_ge(sem(f"d_Z{d}"), r + 1)
                    pe.wait_ge(sem(f"inv{d}"), LEVELS * (r + 1))
                    b = take(pe, f"SA{r}{d}", 6 + d)
                    for h in range(4):
                        last = mm(bank(b)[:, h * 64:(h + 1) * 64], Yi[d][:, h % 2, h // 2, :],
                                  Zs[d][:, h * 64:(h + 1) * 64])
                    give(last, b)
                for d in range(2):
                    g = ORDER[d][r]
                    pe.wait_ge(sem(f"d_SA{d}"), r + 1)
                    pe.wait_ge(sem(f"d_KB{d}"), r + 1)
                    b = take(pe, f"YU{r}{d}", 6 + d)
                    if g >= NCTX:
                        for t in range(2):
                            mm(bank(b)[:, t * P:(t + 1) * P], AR[d][:, t, g, 1, :], Zst[d][:, t, :], True, False,
                               skip_group_check=True)
                            for hp in range(2):
                                h = 2 * t + hp
                                mm(bank(b)[:, h * 64:(h + 1) * 64], KAR[d][:, hp, t, P:2 * P],
                                   Vt[:, g, h * 64:(h + 1) * 64], False, False, skip_group_check=True)
                                last = mm(bank(b)[:, h * 64:(h + 1) * 64], BAR[d][:, hp, t, P:2 * P],
                                          SAs[d][:, h * 64:(h + 1) * 64], False, True, skip_group_check=True)
                    if r < NTILE - 1:
                        for t in range(2):
                            mm(bank(b)[:, 256 + t * P:256 + (t + 1) * P], KB[d][:, 0, t * P:(t + 1) * P],
                               Vt[:, g, t * P:(t + 1) * P], True, False)
                            last = mm(bank(b)[:, 256 + t * P:256 + (t + 1) * P], KB[d][:, 1, t * P:(t + 1) * P],
                                      SAs[d][:, t * P:(t + 1) * P], False, True)
                    give(last, b)
            pe.wait_ge(sem("d_rk"), 1)
            for t in range(2):
                b = take(pe, f"bon{t}", t)
                give(mm(bank(b), mat(BLK), rkA[:, t, :]), b)
                b = take(pe, f"gate{t}", 2 + t)
                give(mm(bank(b), g2s[:, t * P:(t + 1) * P], Dsh[:, 8, CTX:]), b)
            pe.wait_ge(sem("d_gn"), 1)
            for t in range(2):
                b = take(pe, f"db{t}", 4 + t)
                for i in range(NLAT):
                    last = tr(bank(b)[:, i * P:(i + 1) * P], yD[:, i, t * P:(t + 1) * P])
                give(last, b)
            pe.wait_ge(sem("keys"), 32)
            for hh in range(16):
                w_loads = len(range(hh % 3, len(COL_TILES), 4))
                pe.wait_ge(sem(f"w_slot{hh % 3}"), 16 * (w_loads + hh // 3 + 1))
                for q in range(2):
                    b = take(pe, f"wp{hh}{q}", 2 + (2 * hh + q) % 4)
                    for j in range(4):
                        k = 4 * q + j
                        last = mm(bank(b)[:, j * P:(j + 1) * P], wqr[hh % 3][:, k * P:(k + 1) * P],
                                  mat(KEY1 + hh % 2))
                    give(last, b)
            pe.wait_ge(sem("w_out"), 16 * 3)
            pe.wait_ge(sem("y_done"), 4)
            for i in range(NLAT):
                for q in range(2):
                    b = take(pe, f"o{i}{q}", (2 * i + q) % 4)
                    for k in range(KT):
                        last = mm(bank(b), yT[:, k, i * P:(i + 1) * P], w_o[:, k, q * 512:(q + 1) * 512],
                                  k == 0, k == KT - 1)
                    give(last, b)
            def transposed_rows(i):
                pe.wait_ge(sem("f_ready"), i + 1)
                for q in range(2):
                    b = take(pe, f"ft{i}{q}", 4 + q)
                    for j in range(4):
                        k = 4 * q + j
                        last = tr(bank(b)[:, j * P:(j + 1) * P], f_tok[:, i, k * P:(k + 1) * P])
                    give(last, b)
                pe.wait_ge(sem("fT_ready"), 2 * (i + 1))

            def scores(i, n):
                b = take(pe, f"s{i}{n}", 6 + n % 2)
                for k in range(KT):
                    last = mm(bank(b), fT[:, k, :], Wp[:, k, n * 512:(n + 1) * 512], k == 0, k == KT - 1)
                give(last, b)

            transposed_rows(0)
            for n in range(4):
                scores(0, n)
            for i in range(NLAT):
                b0 = 2 * (i % 2)
                for q in range(2):
                    take(pe, f"acc{i}{q}", b0 + q)
                    mm(bank(b0 + q), zmat, zrhs, True, False, skip_group_check=True)
                for part, (h0, h1) in enumerate(HEAD_PARTS):
                    with pe.Fori(0, h1 - h0) as hh:
                        n = i * PH + h0
                        for s in range(TOPK):
                            pe.wait_ge(sem("diag_ready"), hh * TOPK + (n * TOPK + s + 1))
                            pe.wait_ge(sem(f"v_slot{s % 8}"), hh * 32 + (n * 32 + 16 * (s // 8 + 1)))
                            mm(bank(b0), diag[:, s % 2, :], Vr[s % 8][:, 0:512], False, False, skip_group_check=True)
                            mm(bank(b0 + 1), diag[:, s % 2, :], Vr[s % 8][:, 512:], False, False,
                               skip_group_check=True).then_inc(sem("v_used"), 1)
                    if part < 4 and i + 1 < NLAT:
                        if part == 0:
                            transposed_rows(i + 1)
                        scores(i + 1, part)
                for q in range(2):
                    give(mm(bank(b0 + q), zmat, zrhs, False, True, skip_group_check=True), b0 + q)

        @block.sync
        def _(sp):
            def ld(dst, src, s):
                sp.dma_start(dst, src).then_inc(sem(s), 16)

            ld(mats[:, 0:NMAT, :], A["mats"], "consts")
            ld(csil, A["cc"], "cc")
            ld(cols, A["cols"], "cols")
            ld(Xst[0], A["ctx"][0:P, :], "x0")
            ld(adaA[0], A["ada_w"][0], "ada_slot0")
            ld(Xst[1], A["ctx"][P:2 * P, :], "x1")
            ld(adaA[1], A["ada_w"][1], "ada_slot1")
            ld(modA, A["adab_a"], "adab")
            for g in range(2, NTILE):
                ld(Xst[g], A["x"][(g - 2) * P:(g - 1) * P, :], f"x{g}")
                ld(Pst[g - 2], A["pos"][(g - 2) * P:(g - 1) * P, :], f"x{g}")
            for n in (2, 3):
                b, k = use_of[f"adaA{n - 2}"]
                sp.wait_ge(bank_full[b], k)
                ld(adaA[n % 2], A["ada_w"][n], f"ada_slot{n % 2}")
            ld(rows, A["rows"], "params")
            ld(bsb, A["bsb"], "params")
            ld(wsT, A["wsT"], "params")
            ld(wdt, A["wdt"], "params")
            ld(w2s, A["w2"], "params")
            ld(a2s, A["a2"], "params")
            ld(g2s, A["g2"], "params")
            ld(levels_f, A["levels"], "levels")
            ld(mats[:, KEY1, :], A["k1T"], "keys")
            ld(mats[:, KEY2, :], A["k2T"], "keys")
            for g in range(2, NTILE):
                sp.wait_ge(sem("h_sum"), g - 1)
                sp.dma_start(h_dram[(g - 2) * P:(g - 1) * P, :], Xst[g]).then_inc(sem("h_saved"), 16)
            for j in range(len(COL_TILES)):
                if j >= 4:
                    pr = COL_TILES[j - 4][1]
                    b, k = use_of[f"pc{j - 4}" if pr in "cd" else f"p{j - 4}"]
                    sp.wait_ge(bank_full[b], k)
                ld(wring[j % 4], A["w_in"][j], f"w_slot{j % 4}")
            for m, (_, before, loaded, _) in enumerate(ADA_HALVES):
                n, q = m // 2, m % 2
                if m in (0, 1):
                    b, k = use_of[f"pc{len(COL_TILES) - 2 + m}"]
                    sp.wait_ge(bank_full[b], k)
                elif before is not None:
                    sp.wait_ge(sem("adaB_used"), before + 1)
                elif m >= 8:
                    b, k = use_of["cb1"]
                    sp.wait_ge(bank_full[b], k)
                ld(adaB[m], A["ada_w"][4 + n][:, 4 * q:4 * q + 4, :], loaded)
                if m == 1:
                    for row in range(2):
                        ld(mod_row[row][0:1, :], A["adab_b"][:, row, :], f"adaB_bias{row}")
                if q == 0 and n >= 2:
                    sp.wait_ge(sem("mod_saved"), 16 * (n - 1))
                    ld(mod_row[n % 2][0:1, :], A["adab_b"][:, n, :], f"adaB_bias{n % 2}")
                if q == 1 and n >= 1:
                    sp.wait_ge(sem("mod_row"), n)
                    sp.dma_start(mod_dram[:, (n - 1) * 512:n * 512], mod_row[(n - 1) % 2][0:1, :])\
                        .then_inc(sem("mod_saved"), 16)
            sp.wait_ge(sem("mod_row"), 8)
            sp.dma_start(mod_dram[:, 7 * 512:8 * 512], mod_row[1][0:1, :]).then_inc(sem("mod_saved"), 16)
            sp.wait_ge(sem("mod_saved"), 16 * 8)
            sp.wait_ge(sem("d_prep"), 2)
            ld(w_o[:, 1:6, :], A["w_out"][:, 1:6, :], "w_out")
            sp.wait_ge(sem("d_rounds"), 1)
            for hh in range(16):
                if hh >= 3:
                    b, k = use_of[f"wp{hh - 3}1"]
                    sp.wait_ge(bank_full[b], k)
                ld(wqr[hh % 3], A["wqT"][hh], f"w_slot{hh % 3}")
            sp.wait_ge(sem("y_done"), 4)
            ld(w_o[:, 0:1, :], A["w_out"][:, 0:1, :], "w_out")
            ld(w_o[:, 6:8, :], A["w_out"][:, 6:8, :], "w_out")
            ld(modBn.rearrange("p n c -> p (n c)"), mod_dram.partition_broadcast(P), "mod_b")
            ld(rowG, A["ffn_g"], "mod_b")
            sp.wait_ge(sem("h_saved"), 16 * NLAT)
            ld(hL, h_dram.rearrange("(i p) d -> p i d", p=P), "h_load")
            for i in range(NLAT):
                sp.wait_ge(sem("h2_ready"), i + 1)
                sp.dma_start(h2_dram[i * P:(i + 1) * P, :], hL[:, i, :]).then_inc(sem("h2_saved"), 16)
            sp.wait_ge(sem("h2_saved"), 16 * NLAT)
            sp.wait_ge(sem("s_ready"), 4 * NLAT)
            ld(hfin, h2_dram.rearrange("(i p) d -> p i d", p=P), "hfin")
            ld(rowF, A["fin_g"], "hfin")
            for i in range(NLAT):
                sp.wait_ge(sem("out_tile"), i + 1)
                sp.dma_start(out[i * P:(i + 1) * P, :], hfin[:, i, :]).then_inc(sem("out_saved"), 16)
            sp.wait_ge(sem("out_saved"), 16 * NLAT)

        @block.scalar
        def _(e):
            a = Engine(e, "act")
            act = e.activation

            def free(b):
                e.sem_inc(bank_free[b], 1)

            def signal(name):
                e.sem_inc(sem(name), 1)

            nstd = [0]

            def std(o, i, scale, eps):
                nstd[0] += 1
                e.wait_ge(sem("var_ready"), nstd[0])
                a.step(act(o, i, ACT.Sqrt, scale=scale, bias=eps))
                signal("std_ready")

            e.wait_ge(sem("cc"), 16)
            a.step(act(csil, csil, ACT.Silu))
            signal("csil")
            e.wait_ge(sem("eps"), 4)
            e.wait_ge(sem("cols"), 16)
            for g in range(NTILE):
                if g < NCTX:
                    e.wait_ge(sem(f"x{g}"), 16)
                else:
                    e.wait_ge(sem("h_sum"), g - 1)
                a.step(act(sqs, Xst[g], ACT.Square, accum_out=stat[:, g:g + 1]))
            a.step(act(stat[:, 8:8 + NTILE], stat[:, 0:NTILE], ACT.Sqrt, scale=1.0 / D, bias=eps_c[:, 0:1]))
            signal("x_std")
            e.wait_ge(sem("gcol"), 1)
            for g in range(NTILE):
                c = 1 if g < NCTX else 0
                for q in range(2):
                    b = full(e, f"xt{g}{q}")
                    for j in range(4):
                        k = 4 * q + j
                        a.do(act(XT[:, k, g * P:(g + 1) * P], bank(b)[:, j * P:(j + 1) * P], ACT.Identity,
                                 scale=gcol[:, k, c:c + 1], bias=modcol[:, k, c:c + 1]))
                    a.sync()
                    free(b)
                    signal("xt_ready")

            def between(j, part):
                for name in BETWEEN.get((j, part), ()):
                    if name == "a_tok":
                        for t in range(2):
                            b = full(e, f"at{t}")
                            a.step(act(At[:, :, t * P:(t + 1) * P], bank(b, NLAT, P), ACT.Copy))
                            free(b)
                        signal("a_tok")
                    elif name == "dt_exp":
                        e.wait_ge(sem("dt_abs"), 1)
                        a.step(act(tmp48b, tmp48b, ACT.Exp, scale=-1.0))
                        a.step(act(aneg, rows[:, 520:528], ACT.Exp))
                        signal("dt_exp")
                    elif name == "c_silu":
                        e.wait_ge(sem("c_taps"), 1)
                        for t in range(6):
                            a.do(act(Cx[:, t, :], Cx[:, t, :], ACT.Silu, bias=col("ccb", t)))
                        a.sync()
                        signal("c_conv")
                    elif name == "c_tok":
                        for t in range(4):
                            dst = (xs_t if t < 2 else B_t)
                            for q in range(2):
                                b = full(e, f"ct{t}{q}")
                                a.step(act(dst[:, 3 * q:3 * q + 3, (t % 2) * P:(t % 2 + 1) * P], bank(b, 3, P),
                                           ACT.Copy))
                                free(b)
                        signal("c_tok")
                    elif name == "a_std":
                        std(lnst[:, 1, 0:4], lnst[:, 0, 0:4], 1.0 / 256, eps_c[:, 3:4])
                    elif name == "a_back":
                        for t in range(2):
                            b = full(e, f"ab{t}")
                            a.step(act(yT[:, t, :], bank(b), ACT.Silu, scale=col("alg", t), bias=col("alb", t)))
                            free(b)
                        signal("y_done")
                    elif name == "b_std":
                        std(lnst[:, 1, 0:4], lnst[:, 0, 0:4], 1.0 / 256, eps_c[:, 3:4])
                        e.wait_ge(sem("dt_1p"), 1)
                        a.step(act(tmp48b, tmp48b, ACT.Ln))
                        signal("dt_ln")
                    elif name == "c_decay":
                        b = full(e, "dec")
                        a.step(act(decs, bank(b)[:, 0:240].rearrange("p (m n) -> p m n", m=5), ACT.Exp))
                        free(b)
                        signal("c_dec")
                    elif name[0] == "G":
                        i = int(name[1])
                        for d in range(2):
                            b = full(e, f"seg{2 * i + d}")
                            if i >= 1:
                                full(e, f"yc{i - 1}")
                            a.step(act(Lm[d], bank(b, HEADS, P), ACT.Exp))
                            free(b)
                            signal("c_L")

            e.wait_ge(sem("pads"), 1)
            e.wait_ge(sem("params"), 16 * 7)
            for j, (_, part) in enumerate(COL_TILES):
                b = full(e, f"p{j}")
                if part == "a":
                    a.step(act(Araw[:, j, :], bank(b), ACT.Sigmoid if j >= 2 else ACT.Copy))
                elif part == "u":
                    a.step(act(ut[:, j - 4, :], bank(b), ACT.Copy))
                elif part in "zv":
                    t = (j - 6) if part == "v" else (j - 14)
                    dst = (vt if part == "v" else zt)[:, :, t * P:(t + 1) * P]
                    a.step(act(dst, bank(b, NLAT, P), ACT.Copy if part == "v" else ACT.Silu))
                elif part == "c":
                    a.step(act(Cp[:, j - 8, 262:774], bank(b), ACT.Copy))
                else:
                    a.step(act(Dp[:, j - 16, 259:771], bank(b), ACT.Copy))
                free(b)
                if part not in "cd":
                    signal("part_" + part)
                between(j, 0)
                if part in "cd":
                    b = full(e, f"pc{j}")
                    if part == "c":
                        a.step(act(Cp[:, j - 8, 2:258], bank(b)[:, 0:CTX], ACT.Copy))
                    else:
                        a.step(act(Dp[:, j - 16, 1:257], bank(b)[:, 0:CTX], ACT.Copy))
                    free(b)
                    signal("part_" + part)
                    between(j, 1)
            def adaln_row(n):
                b = full(e, f"adaB{n}")
                a.step(act(mod_row[n % 2][0:1, :], bank(b)[0:1, :], ACT.Copy))
                free(b)
                signal("mod_row")

            def own_share(tiles):
                for t in tiles:
                    for o, i, n in ((0, 1, CTX), (CTX, 259, SEQ)):
                        a.do(act(Dsh[:, t, o:o + n], Dp[:, t, i:i + n], ACT.Copy, scale=mumid[:, t:t + 1]))

            e.wait_ge(sem("c_areas_dead"), 1)
            own_share(range(4))
            std(lnst[:, 1, 0:4], lnst[:, 0, 0:4], 1.0 / 256, eps_c[:, 0:1])
            own_share(range(4, 9))
            a.sync()
            signal("d_mid")
            for n in range(3):
                adaln_row(n)
            for t in range(2):
                b = full(e, f"cb{t}")
                a.step(act(yT[:, 4 + t, :], bank(b), ACT.Copy, scale=col("cng", t)))
                free(b)
            signal("y_done")
            e.wait_ge(sem("d_shift"), 1)
            a.step(act(Dsh[:, 6, :], Dsh[:, 6, :], ACT.Tanh))
            a.step(act(Dsh[:, 8, :], Dsh[:, 8, :], ACT.Sigmoid))
            signal("d_tanh")
            adaln_row(3)
            for d in range(2):
                if d == 1:
                    e.wait_ge(sem("d_prep"), 1)
                for kind, dst, bias in (("w", sw, "w0"), ("a", aA, "a0")):
                    for t in range(2):
                        b = full(e, f"l{kind}{d}{t}")
                        a.step(act(dst[:, t, CTX:], bank(b), ACT.Sigmoid, bias=col(bias, 2 * d + t)))
                        free(b)
                        b = full(e, f"lc{kind}{d}{t}")
                        a.step(act(dst[:, t, 0:CTX], bank(b)[:, 0:CTX], ACT.Sigmoid, bias=col(bias, 2 * d + t)))
                        free(b)
                signal("d_sw")
                if d == 0:
                    e.wait_ge(sem("d_kksq"), 1)
                    for t in range(2):
                        b = full(e, f"kn{t}")
                        a.step(act(Wx[:, t, CTX:], bank(b), ACT.Sqrt, bias=eps_c[:, 1:2]))
                        free(b)
                        b = full(e, f"knc{t}")
                        a.step(act(Wx[:, t, 0:CTX], bank(b)[:, 0:CTX], ACT.Sqrt, bias=eps_c[:, 1:2]))
                        free(b)
                    signal("d_kkn")
                e.wait_ge(sem("d_cen"), d + 1)
                wv = Wx.rearrange("p c (g t) -> p c g t", g=NTILE)
                cv = cen.rearrange("p c (g t) -> p c g t", g=NTILE)
                a.step(act(qa[:, d], wv[:, :, :, 0], ACT.Exp, scale=LOGW))
                a.step(act(qb[:, d], cv[:, :, :, P - 1], ACT.Exp, scale=-LOGW))
                for n, (src, sg) in enumerate(((Wx, -LOGW), (cen, -LOGW), (cen, LOGW)) if d == 0 else
                                              ((cen, LOGW), (Wx, LOGW), (Wx, -LOGW))):
                    if 3 * d + n:
                        e.wait_ge(sem("d_exused"), 3 * d + n)
                    a.step(act(Ex, src, ACT.Exp, scale=sg))
                    signal("d_ex")
                    if d == 0 and n < 2:
                        adaln_row(4 + n)
            adaln_row(6)
            adaln_row(7)
            for q in range(3):
                b = full(e, f"vt{q}")
                a.step(act(Vt[:, 2 * q:2 * q + 2, :], bank(b, 2, 256), ACT.Copy))
                free(b)
                signal("d_vt")
            for r in range(NTILE):
                for d in range(2):
                    b = full(e, f"kbt{r}{d}")
                    a.do(act(KB[d][:, 0, :], bank(b)[:, 0:256], ACT.Copy))
                    a.do(act(KB[d][:, 1, :], bank(b)[:, 256:512], ACT.Copy, scale=-1.0))
                    a.sync()
                    free(b)
                    signal(f"d_KB{d}")
                for lv in range(1, LEVELS):
                    for d in range(2):
                        b = full(e, f"R{r}{d}{lv}")
                        a.step(act(Ri[d].rearrange("p a b c -> p (a b c)"), bank(b), ACT.Copy))
                        free(b)
                        signal(f"invR{d}")
                for d in range(2):
                    b = full(e, f"Z{r}{d}")
                    a.step(act(Zs[d], bank(b)[:, 0:256], ACT.Copy))
                    free(b)
                    signal(f"d_Z{d}")
                for d in range(2):
                    b = full(e, f"SA{r}{d}")
                    a.step(act(SAs[d], bank(b)[:, 0:256], ACT.Copy))
                    free(b)
                    signal(f"d_SA{d}")
            for t in range(2):
                b = full(e, f"gate{t}")
                a.step(act(gD[:, t, :], bank(b), ACT.Copy))
                free(b)
            signal("d_gate")
            std(lnst[:, 1, :], lnst[:, 0, :], 1.0 / 64, eps_c[:, 2:3])
            for t in range(2):
                b = full(e, f"db{t}")
                a.step(act(yT[:, 6 + t, :], bank(b), ACT.Identity, scale=col("gng", t), bias=col("gnb", t)))
                free(b)
            signal("d_back")
            for hh in range(16):
                for q in range(2):
                    b = full(e, f"wp{hh}{q}")
                    a.step(act(Wp[:, 4 * q:4 * q + 4, hh * P:(hh + 1) * P], bank(b, 4, P), ACT.Copy))
                    free(b)
            signal("wp_ready")
            for i in range(NLAT):
                e.wait_ge(sem("h2_ready"), i + 1)
                a.step(act(osq, hL[:, i, :], ACT.Square, accum_out=stat[:, i:i + 1]))
                a.step(act(stat[:, 8 + i:9 + i], stat[:, i:i + 1], ACT.Sqrt, scale=1.0 / D, bias=eps_c[:, 0:1]))
                signal("f_std")
            def transposed_rows(i):
                for q in range(2):
                    b = full(e, f"ft{i}{q}")
                    a.step(act(fT[:, 4 * q:4 * q + 4, :], bank(b, 4, P), ACT.Copy))
                    free(b)
                    signal("fT_ready")

            def scores(i, n):
                b = full(e, f"s{i}{n}")
                a.step(act(s_all[:, i, 2 * n:2 * n + 2, :, :].rearrange("p a b c -> p (a b c)"), bank(b), ACT.Copy))
                free(b)
                signal("s_ready")

            def gates(n):
                e.wait_ge(sem("u_used"), n * TOPK + TOPK)
                act(gel[:, :], dots[:, :], ACT.Gelu_apprx_tanh).then_inc(sem("gates"), 1)
                act(egate[:, :], top_all[:, bass.ds(n * 16, 16)], ACT.Exp, accum_out=esum[:, 0:1])\
                    .then_inc(sem("gates"), 1)

            def diagonals(n):
                e.wait_ge(sem("act_ready"), n + 1)
                act(act_cur[:, :], act_all[:, bass.ds(n * 16, 16)], ACT.Copy).then_inc(sem("cur"), 1)
                e.wait_ge(sem("cur"), n + 1)
                for s in range(TOPK):
                    if s >= 2:
                        e.wait_ge(sem("v_used"), n * TOPK + (s - 1))
                    act(diag[:, s % 2, :], mat(IDENT), ACT.Copy, scale=act_cur[:, s:s + 1])\
                        .then_inc(sem("diag_ready"), 1)
                e.wait_ge(sem("v_used"), n * TOPK + TOPK)

            transposed_rows(0)
            e.wait_ge(sem("h2_saved"), 16 * NLAT)
            e.wait_ge(sem("f_ready"), NLAT)
            for n in range(4):
                scores(0, n)
            gates(0)
            for i in range(NLAT):
                for part, (h0, h1) in enumerate(HEAD_PARTS):
                    with e.Fori(0, h1 - h0 - (1 if i == NLAT - 1 and part == 4 else 0)) as hh:
                        n = i * PH + h0
                        e.wait_ge(sem("act_ready"), hh + (n + 1))
                        gates(hh + (n + 1))
                        diagonals(hh + n)
                    if part < 4 and i + 1 < NLAT:
                        if part == 0:
                            transposed_rows(i + 1)
                        scores(i + 1, part)
                if i == NLAT - 1:
                    e.wait_ge(sem("fin_sum"), 1)
                    a.step(act(stat[:, 8:11], stat[:, 0:3], ACT.Sqrt, scale=1.0 / D, bias=eps_c[:, 0:1]))
                    signal("fin_std")
                    diagonals(NH - 1)
                for q in range(2):
                    b = full(e, f"acc{i}{q}")
                    a.step(act(accS[:, i, q * 512:(q + 1) * 512], bank(b), ACT.Copy))
                    free(b)
                signal("acc_ready")
            e.wait_ge(sem("fin_sum"), 2)
            a.step(act(stat[:, 11:12], stat[:, 3:4], ACT.Sqrt, scale=1.0 / D, bias=eps_c[:, 0:1]))
            signal("fin_std")

        @block.gpsimd
        def _(e):
            e.iota(iota16[:, :], pattern=[[1, 16]], base=0, channel_multiplier=0,
                   allow_small_or_imprecise_dtypes=True).then_inc(sem("iota"), 1)
            e.memset(zmat, 0.0).then_inc(sem("iota"), 1)

            def indices(n, idx, par, copied, used):
                e.wait_ge(sem("idx_ready"), n + 1)
                if not isinstance(n, int) or n > 0:
                    e.sem_inc(sem("pool_tick"), 1)
                    e.wait_ge(sem(used), n * TOPK - 4)
                    e.sem_inc(sem("pool_tick"), 1)
                e.tensor_copy(idx[:, par, :], idx_all[:, bass.ds(n * 16, 16)]).then_inc(sem(copied), 1)
                e.wait_ge(sem(copied), n + 1)
                e.sem_inc(sem("pool_tick"), 1)

            def four_rows(n, g, idx, par, ring, slot, table, used):
                if g and not (isinstance(n, int) and n == 0 and g < 2):
                    e.wait_ge(sem(used), n * TOPK + (4 * g - 4))
                    e.sem_inc(sem("pool_tick"), 1)
                for s in range(4 * g, 4 * g + 4):
                    e.indirect_dma_start(ring[s % 8], None, table,
                                         bass.IndirectOffsetOnAxis(ap=idx[:, par, s:s + 1], axis=0))\
                        .then_inc(sem(f"{slot}{s % 8}"), 16)

            def u_rows(n, par, g):
                if g == 0:
                    indices(n, idxU, par, "idxU_copied", "u_used")
                four_rows(n, g, idxU, par, Ur, "u_slot", A["peer_u"], "u_used")

            def v_rows(n, par, g):
                if g == 0:
                    indices(n, idxV, par, "idxV_copied", "v_used")
                four_rows(n, g, idxV, par, Vr, "v_slot", A["peer_v"], "v_used")

            def rows(n, par):
                for g in range(4):
                    u_rows(n + 2, par, g)
                    v_rows(n, par, g)

            for n in range(2):
                for g in range(4):
                    u_rows(n, n, g)
            rows(0, 0)
            with e.Fori(0, (NH - 4) // 2) as m:
                rows(2 * m + 1, 1)
                rows(2 * m + 2, 0)
            rows(NH - 3, 1)
            for n in range(2):
                for g in range(4):
                    v_rows(NH - 2 + n, n, g)

        @block.vector
        def _(e):
            v = Engine(e, "dve")

            def free(b):
                e.sem_inc(bank_free[b], 1)

            def signal(name):
                e.sem_inc(sem(name), 1)

            tt, ts, stt, cp = e.tensor_tensor, e.tensor_scalar, e.scalar_tensor_tensor, e.tensor_copy
            red = e.tensor_reduce
            nstd = [0]

            def bc(ap, shape):
                return ap.to_broadcast(shape)

            def reciprocal_std(stats):
                nstd[0] += 1
                signal("var_ready")
                e.wait_ge(sem("std_ready"), nstd[0])
                v.step(e.reciprocal(stats[1], stats[1]))

            def layer_norm(x, sq, stats, width, centred=True):
                shape = [P, x.shape[1], width]
                if centred:
                    v.step(red(stats[0], x, AX.X, ALU.add))
                    v.step(ts(stats[0], stats[0], 1.0 / width, None, ALU.mult))
                    v.step(tt(x, x, bc(stats[0].unsqueeze(2), shape), ALU.subtract))
                v.step(tt(sq, x, x, ALU.mult))
                v.step(red(stats[0], sq, AX.X, ALU.add))
                reciprocal_std(stats)
                v.step(tt(x, x, bc(stats[1].unsqueeze(2), shape), ALU.mult))

            for j, val in enumerate((EPS, 1e-12, 64e-5, 1e-5)):
                e.memset(eps_c[:, j:j + 1], val).then_inc(sem("eps"), 1)
            e.wait_ge(sem("csil"), 1)
            for k in range(KT):
                v.do(cp(silA[:, k, 0:64], bc(csil[:, k, 0:1], [P, 64])))
                v.do(cp(silA[:, k, 64:P], bc(csil[:, k, 1:2], [P, 64])))
            v.sync()
            signal("sil_a")
            for g in range(NCTX, NTILE):
                e.wait_ge(sem(f"x{g}"), 32)
                v.step(tt(Xst[g], Xst[g], Pst[g - 2], ALU.add))
                signal("h_sum")
            e.wait_ge(sem("adab"), 16)
            e.wait_ge(sem("x_std"), 1)
            v.step(e.reciprocal(stat[:, 8:8 + NTILE], stat[:, 8:8 + NTILE]))
            for g in range(2):
                v.step(ts(XN[g], Xst[g], stat[:, 8 + g:9 + g], None, ALU.mult))
                signal("xn")
            for n in range(4):
                b = full(e, f"adaA{n}")
                v.step(tt(modA[:, n, :], modA[:, n, :], bank(b), ALU.add))
                free(b)
                signal("mod_a")
            for n in range(4):
                b = full(e, f"mc{n}")
                v.step(cp(modcol[:, 4 * n:4 * n + 4, :], bank(b, 4, 2, 64)[:, :, :, 0]))
                free(b)
            v.step(ts(gcol, modcol[:, 8:16, :], 1.0, None, ALU.add))
            v.step(tt(gcol, gcol, bc(colr("mixg").unsqueeze(2), [P, 8, 2]), ALU.mult))
            signal("gcol")
            for g in range(2, NTILE):
                full(e, f"xt{g - 2}1")
                v.step(ts(XN[g % 2], Xst[g], stat[:, 8 + g:9 + g], None, ALU.mult))
                signal("xn")
            e.wait_ge(sem("h_saved"), 16 * NLAT)
            e.wait_ge(sem("xt_ready"), 2 * NTILE)
            e.wait_ge(sem("levels"), 16)
            v.step(cp(levels[:, :, :], levels_f))
            v.do(e.memset(Apad, 0.0))
            v.do(e.memset(Cp, 0.0))
            v.do(e.memset(Dp, 0.0))
            v.do(e.memset(scanm, 1.0))
            v.sync()
            v.step(e.memset(scanm.rearrange("p (g t) -> p g t", g=NTILE)[:, :, 0:1], 0.0))
            signal("pads")
            e.wait_ge(sem("part_a"), 4)
            v.step(tt(Apad[:, :, 15:15 + SEQ], Araw[:, 0:2, :], Araw[:, 2:4, :], ALU.mult))
            for k in range(TAPS_A):
                for t in range(2):
                    w = cols[:, COLS["acw"][0] + 2 * k + t:COLS["acw"][0] + 2 * k + t + 1]
                    if k == 0:
                        v.do(ts(Ah[:, t, :], Apad[:, t, 0:SEQ], w, col("acb", t), ALU.mult, ALU.add))
                    else:
                        v.e.wait_ge(v.done, v.n - 1)
                        v.do(stt(Ah[:, t, :], Apad[:, t, k:k + SEQ], w, Ah[:, t, :], ALU.mult, ALU.add))
            v.sync()
            signal("a_conv")
            e.wait_ge(sem("params"), 16 * 7)
            b = full(e, "dt")
            v.step(tt(tmp48.rearrange("p (g n) -> p g n", n=8), bank(b)[:, 0:48].rearrange("p (g n) -> p g n", n=8),
                      bc(rows[:, 512:520].unsqueeze(1), [P, NTILE, 8]), ALU.add))
            free(b)
            v.step(stt(tmp48b, tmp48, -1.0, tmp48, ALU.mult, ALU.max))
            signal("dt_abs")
            e.wait_ge(sem("part_c"), 6)
            for t in range(6):
                for k in range(TAPS_C):
                    w = cols[:, COLS["ccw"][0] + 6 * k + t:COLS["ccw"][0] + 6 * k + t + 1]
                    if k:
                        v.sync()
                    for o, i, n in ((0, 0, CTX), (CTX, 260, SEQ)):
                        dst, src = Cx[:, t, o:o + n], Cp[:, t, i + k:i + k + n]
                        if k == 0:
                            v.do(ts(dst, src, w, None, ALU.mult))
                        else:
                            v.do(stt(dst, src, w, dst, ALU.mult, ALU.add))
            v.sync()
            signal("c_taps")
            st4 = (lnst[:, 0, 0:4], lnst[:, 1, 0:4])
            e.wait_ge(sem("a_tok"), 1)
            layer_norm(At, Asq, st4, 256)
            signal("a_norm")
            e.wait_ge(sem("dt_exp"), 1)
            v.step(ts(tmp48b, tmp48b, 1.0, None, ALU.add))
            signal("dt_1p")
            v.step(ts(aneg, aneg, -1.0, None, ALU.mult))
            e.wait_ge(sem("part_v"), 2)
            layer_norm(vt, Bsq, st4, 256)
            v.step(tt(vt, vt, bc(rows[:, 0:256].unsqueeze(1), [P, NLAT, 256]), ALU.mult))
            v.step(tt(vt, vt, bc(rows[:, 256:512].unsqueeze(1), [P, NLAT, 256]), ALU.add))
            signal("b_norm")
            e.wait_ge(sem("dt_ln"), 1)
            v.step(stt(dts, tmp48, 0.0, tmp48b, ALU.max, ALU.add))
            v.step(tt(das.rearrange("p (g n) -> p g n", n=8), dts.rearrange("p (g n) -> p g n", n=8),
                      bc(aneg.unsqueeze(1), [P, NTILE, 8]), ALU.mult))
            signal("c_da")
            dv = lambda x, d: x.rearrange("p (g d h) -> p g d h", d=2, h=HEADS)[:, :, d, :]
            e.wait_ge(sem("c_tok"), 1)
            heads = lambda x: x.rearrange("p g (h e) -> p g h e", h=HEADS)
            for d in range(2):
                v.do(tt(heads(xdt[d]), heads(xs_t)[:, NCTX:], bc(dv(dts, d)[:, NCTX:].unsqueeze(3), [P, NLAT, HEADS, 64]),
                        ALU.mult))
            e.wait_ge(sem("c_dec"), 1)
            for d in range(2):
                v.step(tt(dv(cst, d), dv(dts, d), dv(decs[:, 1 + 2 * d, :], d), ALU.mult))
                v.do(tt(heads(xst[d]), heads(xs_t), bc(dv(cst, d).unsqueeze(3), [P, NTILE, HEADS, 64]), ALU.mult))
            v.sync()
            signal("c_xst")
            for t in range(2):
                b = full(e, f"bm{t}")
                v.step(tt(Bmix[:, t], bank(b, NLAT, P), bc(bsb[:, t, :].unsqueeze(1), [P, NLAT, P]), ALU.add))
                free(b)
                v.step(tt(yT[:, 2 + t, :], Bmix[:, t].rearrange("p a b -> p (a b)"), ut[:, t, :], ALU.mult))
            signal("y_done")

            def decay_rhs(i):
                for d in range(2):
                    if i >= 1:
                        full(e, f"seg{2 * (i - 1) + d}")
                    v.step(tt(seg[d], bc(mat((LE, GE)[d]).unsqueeze(1), [P, HEADS, P]),
                              bc(dv(das, d)[:, NCTX + i, :].unsqueeze(2), [P, HEADS, P]), ALU.mult))
                    signal("c_segrhs")

            def chunk_scores(i):
                b = full(e, f"G{i}")
                for d in range(2):
                    v.do(tt(Gm[d][:, i], bank(b, 2, P), bc(mat((LE, GE)[d]).unsqueeze(1), [P, 2, P]), ALU.mult))
                v.sync()
                free(b)
                if i < NLAT - 1:
                    decay_rhs(i + 1)
                for d in range(2):
                    e.wait_ge(sem("c_L"), 2 * i + d + 1)
                    v.step(tt(Lm[d].rearrange("p (g h) l -> p g h l", g=2), Lm[d].rearrange("p (g h) l -> p g h l", g=2),
                              bc(Gm[d][:, i].unsqueeze(2), [P, 2, 2, P]), ALU.mult))
                    signal("c_M")

            def chunk_outputs(i):
                b = full(e, f"yc{i}")
                y = yC[:, i, :]
                v.step(cp(y, bank(b)[:, 0:256]) if i not in begun else tt(y, y, bank(b)[:, 0:256], ALU.add))
                begun.add(i)
                free(b)

            def chunk_state(step):
                for d in range(2):
                    g = ORDER[d][step]
                    if g >= NCTX:
                        y, new = yC[:, g - NCTX, :], g - NCTX not in begun
                        begun.add(g - NCTX)
                        b = full(e, f"yo{d}{g}")
                        v.step(tt(h64(y if new else Ctmp), h64(bank(b)[:, 0:256]),
                                  bc(dv(decs[:, 2 * d, :], d)[:, g, :].unsqueeze(2), [P, HEADS, 64]), ALU.mult))
                        free(b)
                        if not new:
                            v.step(tt(y, y, Ctmp, ALU.add))
                    if step < NTILE - 1:
                        b = full(e, f"cu{d}{step}")
                        if step == 0:
                            v.step(cp(Sc[d], bank(b)[:, 0:256]))
                        else:
                            v.step(tt(h64(Sc[d]), h64(Sc[d]),
                                      bc(dv(decs[:, 4, :], d)[:, g, :].unsqueeze(2), [P, HEADS, 64]), ALU.mult))
                            v.step(tt(Sc[d], Sc[d], bank(b)[:, 0:256], ALU.add))
                        free(b)
                        signal(f"c_state{d}")

            begun = set()
            h64 = lambda x: x.rearrange("p (h e) -> p h e", h=HEADS)
            v.step(tt(mumid, colr("mup"), colr("mun"), ALU.add))
            v.step(ts(mumid, mumid, -1.0, 1.0, ALU.mult, ALU.add))
            decay_rhs(0)
            chunk_scores(0)
            chunk_state(0)
            chunk_state(1)
            for i in range(NLAT):
                chunk_outputs(i)
                if i < NLAT - 1:
                    chunk_scores(i + 1)
                chunk_state(i + 2)
            v.step(tt(heads(Csq), heads(xs_t)[:, NCTX:],
                      bc(rows[:, 528:532].unsqueeze(1).unsqueeze(3), [P, NLAT, HEADS, 64]), ALU.mult))
            signal("c_areas_dead")
            v.step(tt(yC, yC, Csq, ALU.add))
            v.step(tt(yC, yC, zt, ALU.mult))
            layer_norm(yC, Csq, st4, 256, centred=False)
            signal("c_norm")
            e.wait_ge(sem("d_mid"), 1)
            for t in range(9):
                for sh, w in ((-1, col("mup", t)), (1, col("mun", t))):
                    v.sync()
                    for o, i, n in ((0, 1, CTX), (CTX, 259, SEQ)):
                        dst = Dsh[:, t, o:o + n]
                        v.do(stt(dst, Dp[:, t, i + sh:i + sh + n], w, dst, ALU.mult, ALU.add))
            v.sync()
            signal("d_shift")
            r_, k_, v_ = Dsh[:, 0:2, :], Dsh[:, 2:4, :], Dsh[:, 4:6, :]
            full(e, "cb1")
            for t in range(2):
                v.do(ts(kkA[:, t, :], k_[:, t, :], col("kk", t), None, ALU.mult))
            v.step(ts(kam1, colr("ka"), -1.0, 1.0, ALU.mult, ALU.add))
            v.step(tt(Ex, kkA, kkA, ALU.mult))
            signal("d_kksq")
            g6 = lambda x: x.rearrange("p c (g t) -> p c g t", g=NTILE)
            for d in range(2):
                e.wait_ge(sem("d_sw"), d + 1)
                if d == 0:
                    e.wait_ge(sem("d_kkn"), 1)
                    v.step(e.reciprocal(Wx, Wx))
                    v.step(tt(kkA, kkA, Wx, ALU.mult))
                for t in range(2):
                    v.do(e.tensor_tensor_scan(cen[:, t, :], scanm, sw[:, t, :], 0.0, ALU.mult, ALU.add))
                for t in range(2):
                    v.do(ts(kdA[:, t, :], aA[:, t, :], col("ka", t), kam1[:, t:t + 1], ALU.mult, ALU.add))
                v.sync()
                v.do(tt(kdA, kdA, k_, ALU.mult))
                v.do(tt(aA, aA, kkA, ALU.mult))
                v.step(cp(cmid, g6(cen)[:, :, :, 63]))
                for t in range(2):
                    v.do(tt(g6(cen)[:, t], g6(cen)[:, t], bc(cmid[:, t, :].unsqueeze(2), [P, NTILE, P]), ALU.subtract))
                v.sync()
                v.do(tt(Wx, cen, sw, ALU.subtract))
                v.step(cp(kds, kdA[:, :, CTX:]) if d == 0 else tt(kds, kds, kdA[:, :, CTX:], ALU.add))
                signal("d_cen")
                for n in range(3):
                    e.wait_ge(sem("d_ex"), 3 * d + n + 1)
                    if n < 2:
                        for t in range(2):
                            v.do(tt(AR[d][:, t, :, n, :], g6(kkA if n == 0 else r_)[:, t], g6(Ex)[:, t], ALU.mult))
                    else:
                        v.do(tt(Bt[d], aA, Ex, ALU.mult))
                        v.do(tt(Kt[d], kdA, Ex, ALU.mult))
                    v.sync()
                    signal("d_exused")
                signal("d_prep")
                pre, post = (qa, qb) if d == 0 else (qb, qa)
                for r in range(NTILE - 1):
                    v.do(tt(qs[:, d, :, r:r + 1], post[:, d, :, ORDER[d][r]:ORDER[d][r] + 1],
                            pre[:, d, :, ORDER[d][r + 1]:ORDER[d][r + 1] + 1], ALU.mult))
                v.sync()
            full(e, "adaB7")
            for r in range(NTILE):
                for d in range(2):
                    g = ORDER[d][r]
                    mask = mats[:, (LT, GT)[d]:(LT, GT)[d] + 2, :].rearrange("p a b -> p (a b)")
                    neg = mats[:, (NLT, NGT)[d]:(NLT, NGT)[d] + 2, :].rearrange("p a b -> p (a b)")
                    for hp in range(2):
                        b = full(e, f"kar{r}{d}{hp}")
                        v.step(tt(KAR[d][:, hp], bank(b, 2, 256), bc(mask.unsqueeze(1), [P, 2, 256]), ALU.mult))
                        free(b)
                    for hp in range(2):
                        b = full(e, f"bar{r}{d}{hp}")
                        v.step(tt(BAR[d][:, hp], bank(b, 2, 256), bc(neg.unsqueeze(1), [P, 2, 256]), ALU.mult))
                        free(b)
                    for hp in range(2):
                        b = full(e, f"na{r}{d}{hp}")
                        v.step(tt(NA[d][:, hp], bank(b, 2, P), bc(mat((NGT, NLT)[d]).unsqueeze(1), [P, 2, P]),
                                  ALU.mult))
                        free(b)
                    q4 = lambda x: x.rearrange("p a b c -> p (a b) c")
                    v.do(cp(q4(Xi[d]), bc(mat(IDENT).unsqueeze(1), [P, 4, P])))
                    v.do(cp(q4(Yi[d]), bc(mat(IDENT).unsqueeze(1), [P, 4, P])))
                    v.sync()
                    lx, ly = LEVELS * d, LEVELS * (1 - d)
                    v.do(e.copy_predicated(q4(Xi[d]), bc(levels[:, lx, :].unsqueeze(1), [P, 4, P]), q4(NA[d])))
                    for hp in range(2):
                        v.do(e.copy_predicated(Yi[d][:, hp], bc(levels[:, ly, :].unsqueeze(1), [P, 2, P]),
                                               BAR[d][:, hp, :, 0:P]))
                    v.sync()
                    signal(f"inv{d}")
                for lv in range(1, LEVELS):
                    for d in range(2):
                        lx, ly = LEVELS * d + lv, LEVELS * (1 - d) + lv
                        b2 = full(e, f"PY{r}{d}{lv}")
                        if lv < LEVELS - 1:
                            b1 = full(e, f"PX{r}{d}{lv}")
                            v.do(e.copy_predicated(q4(Xi[d]), bc(levels[:, lx, :].unsqueeze(1), [P, 4, P]),
                                                   bank(b1, 4, P)))
                        v.do(e.copy_predicated(q4(Yi[d]), bc(levels[:, ly, :].unsqueeze(1), [P, 4, P]),
                                               bank(b2, 4, P)))
                        v.sync()
                        if lv < LEVELS - 1:
                            free(b1)
                        free(b2)
                        signal(f"inv{d}")
                for d in range(2):
                    g = ORDER[d][r]
                    b = full(e, f"YU{r}{d}")
                    if r < NTILE - 1:
                        for t in range(2):
                            v.do(stt(T1[d][:, t, :], bank(b)[:, 256 + t * P:256 + (t + 1) * P], qs[:, d, t, r:r + 1],
                                     mat(BLK), ALU.mult, ALU.mult))
                        v.sync()
                        for t in range(2):
                            if r == 0:
                                v.do(cp(Zst[d][:, t, :], T1[d][:, t, :]))
                            else:
                                v.do(stt(Zst[d][:, t, :], Zst[d][:, t, :], qs[:, d, t, r:r + 1], T1[d][:, t, :],
                                         ALU.mult, ALU.add))
                        v.sync()
                        signal(f"d_state{d}")
                    if g >= NCTX:
                        first = (g - NCTX < 2) == (d == 0)
                        y = yD[:, g - NCTX, :]
                        v.step(cp(y, bank(b)[:, 0:256]) if first else tt(y, y, bank(b)[:, 0:256], ALU.add))
                    free(b)
            signal("d_rounds")
            e.wait_ge(sem("d_vt"), 3)
            for t in range(2):
                v.do(stt(rkA[:, t, :], r_[:, t, CTX:], col("rk", t), kds[:, t, :], ALU.mult, ALU.mult))
            v.sync()
            signal("d_rk")
            for t in range(2):
                b = full(e, f"bon{t}")
                v.step(tt(bon[:, t, :], bank(b), v_[:, t, CTX:], ALU.mult))
                free(b)
            layer_norm(yD.rearrange("p i (h e) -> p (i h) e", e=64), Dsq.rearrange("p i (h e) -> p (i h) e", e=64),
                       (lnst[:, 0, :], lnst[:, 1, :]), 64)
            signal("d_gn")
            e.wait_ge(sem("d_gate"), 1)
            e.wait_ge(sem("d_back"), 1)
            v.step(tt(yT[:, 6:8, :], yT[:, 6:8, :], bon, ALU.add))
            v.step(tt(yT[:, 6:8, :], yT[:, 6:8, :], gD, ALU.mult))
            signal("y_done")
            e.wait_ge(sem("mod_b"), 32)
            v.step(ts(modB[:, 2, :], modB[:, 2, :], 1.0, None, ALU.add))
            v.step(tt(modB[:, 2, :], modB[:, 2, :], rowG, ALU.mult))
            v.step(cp(gate2, modB[:, 3, :]))

            def ffn_input(i):
                e.wait_ge(sem("f_std"), i + 1)
                v.step(e.reciprocal(stat[:, 8 + i:9 + i], stat[:, 8 + i:9 + i]))
                v.step(stt(f_tok[:, i, :], hL[:, i, :], stat[:, 8 + i:9 + i], modB[:, 2, :], ALU.mult, ALU.mult))
                v.step(tt(f_tok[:, i, :], f_tok[:, i, :], modB[:, 1, :], ALU.add))
                signal("f_ready")

            e.wait_ge(sem("h_load"), 16)
            for i in range(NLAT):
                for q in range(2):
                    sl = slice(q * 512, (q + 1) * 512)
                    b = full(e, f"o{i}{q}")
                    v.step(tt(ytmp, bank(b), modB[:, 0, sl], ALU.mult))
                    free(b)
                    v.step(tt(hL[:, i, sl], hL[:, i, sl], ytmp, ALU.add))
                signal("h2_ready")
                if i >= 1:
                    ffn_input(i - 1)
            ffn_input(NLAT - 1)
            chain = sem("route_step")
            e.wait_ge(sem("iota"), 2)
            NEG = -3.0e38

            ROUTE_BEFORE, ROUTE_STEPS = (0, 6, 12, 19), 28

            def route(n, m, part):
                k = [ROUTE_BEFORE[part]]

                def step(ins):
                    k[0] += 1
                    ins.then_inc(chain, 1)
                    e.wait_ge(chain, m * ROUTE_STEPS + k[0])
                    e.sem_inc(sem("route_tick"), 1)

                def best16(values, index, x, rest):
                    step(e.max(values[:, 0:8], x))
                    step(e.max_index(index[:, 0:8], values[:, 0:8], x))
                    step(e.match_replace(rest, values[:, 0:8], x, NEG))
                    step(e.max(values[:, 8:16], rest))
                    step(e.max_index(index[:, 8:16], values[:, 8:16], rest))

                if part == 0:
                    sv = s_all.rearrange("p i h a k -> p (i h a k)")
                    step(cp(sc[:, :, :].rearrange("p a k -> p (a k)"), sv[:, bass.ds(n * 256, 256)]))
                    best16(v16[:, 0, :], i16[:, 0, :], sc[:, 0, :], sc2[:, 0, :])
                elif part == 1:
                    best16(v16[:, 1, :], i16[:, 1, :], sc[:, 1, :], sc2[:, 1, :])
                    step(tt(cand.rearrange("p (a b) -> p a b", a=16), bc(v16[:, 0, :].unsqueeze(2), [P, 16, 16]),
                            bc(v16[:, 1, :].unsqueeze(1), [P, 16, 16]), ALU.add))
                elif part == 2:
                    best16(top16, pos, cand, cand2)
                    step(ts(posab[:, 0, :], pos[:, :], 4, None, ALU.logical_shift_right))
                    step(ts(posab[:, 1, :], pos[:, :], 15, None, ALU.bitwise_and))
                else:
                    step(cp(posf[:, :, :], posab[:, :, :]))
                    step(cp(i16f[:, :, :], i16[:, :, :]))
                    for half in range(2):
                        o3 = oh[:, half, :].rearrange("p (a b) -> p a b", a=16)
                        step(tt(o3, bc(posf[:, half, :].unsqueeze(2), [P, 16, 16]),
                                bc(iota16[:, :].unsqueeze(1), [P, 16, 16]), ALU.is_equal))
                        step(tt(o3, o3, bc(i16f[:, half, :].unsqueeze(1), [P, 16, 16]), ALU.mult))
                        step(red(sel[:, half, :], o3, AX.X, ALU.add))
                    step(stt(idx_all[:, bass.ds(n * 16, 16)], sel[:, 0, :], float(NKEY), sel[:, 1, :],
                             ALU.mult, ALU.add))
                    ts(top_all[:, bass.ds(n * 16, 16)], top16[:, :], top16[:, 0:1], None, ALU.subtract)\
                        .then_inc(sem("idx_ready"), 1)
                assert k[0] == (ROUTE_BEFORE + (ROUTE_STEPS,))[part + 1], k[0]

            def dot_products(n, i, g):
                for s in range(4 * g, 4 * g + 4):
                    e.wait_ge(sem(f"u_slot{s % 8}"), n * 32 + 16 * (s // 8 + 1))
                    e.tensor_tensor_reduce(Ur[s % 8], Ur[s % 8], f_tok[:, i, :], 1.0, 0.0, ALU.mult, ALU.add,
                                           dots[:, s:s + 1]).then_inc(sem("u_used"), 1)

            def weights(n):
                e.wait_ge(sem("gates"), n * 2 + 2)
                e.reciprocal(esum[:, 1:2], esum[:, 0:1]).then_inc(sem("inverse_sum"), 1)
                e.wait_ge(sem("inverse_sum"), n + 1)
                stt(act_all[:, bass.ds(n * 16, 16)], gel[:, :], esum[:, 1:2], egate[:, :], ALU.mult, ALU.mult)\
                    .then_inc(sem("act_ready"), 1)

            e.wait_ge(sem("s_ready"), 1)
            def final_sum(i):
                e.wait_ge(sem("acc_ready"), i + 1)
                v.step(tt(accS[:, i, :], accS[:, i, :], gate2, ALU.mult))
                v.step(tt(accS[:, i, :], accS[:, i, :], hfin[:, i, :], ALU.add))
                v.step(e.tensor_tensor_reduce(fsq, accS[:, i, :], accS[:, i, :], 1.0, 0.0, ALU.mult, ALU.add,
                                              stat[:, i:i + 1]))

            for n in range(2):
                for part in range(4):
                    route(n, n, part)
            e.wait_ge(sem("s_ready"), 4)
            for i in range(NLAT):
                last = i == NLAT - 1
                with e.Fori(0, PH - 2) as h:
                    n = h + i * PH
                    for g in range(4):
                        dot_products(n, i, g)
                        route(n + 2, n + 2, g)
                    weights(n)
                if not last:
                    with e.Fori(0, 2) as h:
                        n = h + (i * PH + PH - 2)
                        for g in range(4):
                            dot_products(n, i, g)
                            if g == 0:
                                e.wait_ge(sem("s_ready"), 4 * (i + 2))
                            route(n + 2, n + 2, g)
                        weights(n)
                else:
                    e.wait_ge(sem("hfin"), 32)
                    for t in range(NLAT - 1):
                        final_sum(t)
                    signal("fin_sum")
                    for n in (NH - 2, NH - 1):
                        for g in range(4):
                            dot_products(n, i, g)
                        weights(n)
            e.wait_ge(sem("fin_std"), 1)
            v.step(e.reciprocal(stat[:, 8:11], stat[:, 8:11]))
            for i in range(NLAT):
                if i == NLAT - 1:
                    final_sum(i)
                    signal("fin_sum")
                    e.wait_ge(sem("fin_std"), 2)
                    v.step(e.reciprocal(stat[:, 8 + i:9 + i], stat[:, 8 + i:9 + i]))
                v.step(stt(hfin[:, i, :], accS[:, i, :], stat[:, 8 + i:9 + i], rowF, ALU.mult, ALU.mult))
                signal("out_tile")


def positions():
    grid_w = 64
    row = np.repeat(np.arange(SEQ // grid_w), grid_w).astype(np.float32)
    column = np.tile(np.arange(grid_w), SEQ // grid_w).astype(np.float32)
    q = D // 4
    freq = (10000.0 ** (-np.arange(q, dtype=np.float64) / q)).astype(np.float32)
    ar, ac = row[:, None] * freq, column[:, None] * freq
    return np.concatenate([np.sin(ar), np.cos(ar), np.sin(ac), np.cos(ac)], -1).astype(np.float32)


def constant_matrices():
    p, f = np.arange(P)[:, None], np.arange(P)[None, :]
    one = lambda c: c.astype(np.float32)
    m = [one(p == f), one(p < f), one(p <= f), one(p > f), one(p >= f),
         -one(p < f), -one(p <= f), -one(p > f), -one(p >= f), one(p >= 0) * one(f >= 0), one(p // 64 == f // 64)]
    lower = [((p >> (n + 1)) == (f >> (n + 1))) & ((p >> n) & 1 == 1) & ((f >> n) & 1 == 0) for n in range(LEVELS)]
    lv = np.stack(lower + [x.T for x in lower]).astype(np.float32)
    return np.ascontiguousarray(np.stack(m).transpose(1, 0, 2)), np.ascontiguousarray(lv.transpose(1, 0, 2))


def kernel(**inputs):
    import concourse.bacc as bacc
    from concourse.bass_utils import run_bass_kernel_spmd

    g = {k: np.asarray(v) for k, v in inputs.items()}

    def columns(a):
        return np.reshape(a, (-1, P)).T

    def over_partitions(a):
        return np.broadcast_to(np.reshape(a, (1,) + a.shape), (P,) + a.shape)

    w_in = g["w_in"][0]
    mats, levels = constant_matrices()
    ada_w = g["ada_w"][0].reshape(KT, P, 12, 512).transpose(2, 1, 0, 3)
    ada_b = g["ada_b"][0].reshape(12, 512)
    arrays = {
        "x": g["x"][0], "ctx": g["ctx"][0], "pos": positions(), "mats": mats, "levels": levels,
        "cc": np.stack([g["c"][0], g["c_ctx"]]).reshape(2, KT, P).transpose(2, 1, 0),
        "ada_w": ada_w, "adab_a": over_partitions(ada_b[0:4]), "adab_b": ada_b[4:12][None],
        "cols": np.concatenate([columns(a) for a in (
            g["norm_mix_g"], g["a_conv_w"], g["a_conv_b"], g["a_ln_g"], g["a_ln_b"], g["c_conv_w"], g["c_conv_b"],
            g["d_mu_prev"], g["d_mu_next"], g["d_w0"], g["d_a0"], g["d_k_k"], g["d_k_a"], g["d_r_k"],
            g["d_gn_g"], g["d_gn_b"], g["c_norm_g"])], axis=1),
        "rows": over_partitions(np.concatenate([g["b_ln_g"][0], g["b_ln_b"][0], g["c_dt_bias"][0].reshape(-1),
                                                g["c_a_log"][0].reshape(-1), g["c_d"][0]])),
        "bsb": np.repeat(g["b_bs"][0], 64, axis=0).reshape(2, P, P).transpose(1, 0, 2),
        "wsT": g["b_ws"][0].transpose(2, 0, 1),
        "wdt": w_in[:, OFF_D - 8:OFF_D].reshape(KT, P, 8).transpose(1, 0, 2),
        "w2": g["d_w2"][0].reshape(P, 256), "a2": g["d_a2"][0].reshape(P, 256), "g2": g["d_g2"][0],
        "w_in": np.stack([w_in[:, c:c + P].reshape(KT, P, P).transpose(1, 0, 2) for c, _ in COL_TILES]),
        "w_out": g["w_out"][0].reshape(KT, P, D).transpose(1, 0, 2),
        "wqT": g["peer_wq"][0].T.reshape(16, P, D), "k1T": g["peer_k1"][0].T, "k2T": g["peer_k2"][0].T,
        "ffn_g": over_partitions(g["norm_ffn_g"][0]), "fin_g": over_partitions(g["final_g"]),
        "peer_u": g["peer_u"][0], "peer_v": g["peer_v"][0],
    }
    nc = bacc.Bacc("TRN2", target_bir_lowering=False, num_devices=1)
    in_map, aps = {}, {}
    for name, a in arrays.items():
        a = np.ascontiguousarray(a)
        in_map[f"in_{name}"] = a
        aps[name] = nc.dram_tensor(f"in_{name}", a.shape, mybir.dt.from_np(a.dtype), kind="ExternalInput").ap()
    out = nc.dram_tensor("out_0", (SEQ, D), F32, kind="ExternalOutput").ap()
    build_program(nc, aps, out)
    r = run_bass_kernel_spmd(nc, [in_map], core_ids=[0])
    return np.reshape(r.results[0]["out_0"], (1, SEQ, D))
```
